# Optimizing a Trainium2 kernel written in Bass

```python
import jax, jax.numpy as jnp
from jax import lax
import numpy as np

D_MODEL = 2048
BATCH = 1
SEQ = 512
DEPTH = 1

CHUNK = 64
N_BRANCH = 4
BRANCH_W = D_MODEL // 4
GMLP_BLOCK = 128
GMLP_GROUPS = 4
GMLP_GW = BRANCH_W // GMLP_GROUPS
HEAD_DIM = 64
N_Q_HEADS = BRANCH_W // HEAD_DIM
N_KV_HEADS = 2
Q_PER_KV = N_Q_HEADS // N_KV_HEADS
WINDOW = 128
WIN_CHUNKS = WINDOW // CHUNK
POOL_WINDOWS = (2, 4, 8, 16)
POOL_GROUPS = 4
POOL_GW = BRANCH_W // POOL_GROUPS
POOL_OUT_GW = D_MODEL // POOL_GROUPS
CONV_W = 31
D_FF = -(-8 * D_MODEL // (3 * 256)) * 256
IN_A = 2 * BRANCH_W
IN_B_Q = N_Q_HEADS * HEAD_DIM
IN_B_KV = N_KV_HEADS * HEAD_DIM
IN_B = IN_B_Q + 2 * IN_B_KV
IN_C = BRANCH_W
IN_D = 2 * BRANCH_W
D_IN = IN_A + IN_B + IN_C + IN_D
NEG = float(np.finfo(np.float32).min)

kernel_name = "hybrid_gated_parallel_mixers_chunk_causal"

def rms_norm(x, g, eps=1e-6):
    xf = x.astype(jnp.float32)
    y = xf * lax.rsqrt(jnp.mean(xf * xf, axis=-1, keepdims=True) + eps)
    return (y * g.astype(jnp.float32)).astype(x.dtype)

def layer_norm(x, g, b, eps=1e-5):
    xf = x.astype(jnp.float32)
    mu = jnp.mean(xf, axis=-1, keepdims=True)
    var = jnp.mean(jnp.square(xf - mu), axis=-1, keepdims=True)
    y = (xf - mu) * lax.rsqrt(var + eps)
    return (y * g.astype(jnp.float32) + b.astype(jnp.float32)).astype(x.dtype)

def shift_chunks(t, s):
    if s == 0:
        return t
    return jnp.concatenate([jnp.zeros_like(t[:, :s]), t[:, :-s]], axis=1)

def gmlp_mixer(za, v_g, v_b, w_s, b_s):
    B, S, _ = za.shape
    z = jax.nn.gelu(za, approximate=False)
    u, v = z[..., :BRANCH_W], z[..., BRANCH_W:]
    v = layer_norm(v, v_g, v_b)
    vb = v.reshape(B, S // GMLP_BLOCK, GMLP_BLOCK, GMLP_GROUPS, GMLP_GW)
    pos_chunk = jnp.arange(GMLP_BLOCK) // CHUNK
    mask = pos_chunk[:, None] >= pos_chunk[None, :]
    ws = jnp.where(mask[None], w_s, 0.0)
    sv = jnp.einsum('gij,bnjgc->bnigc', ws, vb) + b_s.T[None, None, :, :, None]
    return u * sv.reshape(B, S, BRANCH_W)

def sliding_window_attention(q, k, v, sinks):
    B, S, _ = q.shape
    nC = S // CHUNK
    q = q.reshape(B, nC, CHUNK, N_KV_HEADS, Q_PER_KV, HEAD_DIM)
    k = k.reshape(B, nC, CHUNK, N_KV_HEADS, HEAD_DIM)
    v = v.reshape(B, nC, CHUNK, N_KV_HEADS, HEAD_DIM)
    shifts = range(WIN_CHUNKS - 1, -1, -1)
    kb = jnp.concatenate([shift_chunks(k, s) for s in shifts], axis=2)
    vb = jnp.concatenate([shift_chunks(v, s) for s in shifts], axis=2)
    scores = jnp.einsum('bnqkgd,bnjkd->bnkgqj', q, kb).astype(jnp.float32) * (HEAD_DIM ** -0.5)
    slot_shift = (WIN_CHUNKS - 1) - jnp.arange(WINDOW) // CHUNK
    valid = jnp.arange(nC)[:, None] >= slot_shift[None, :]
    scores = jnp.where(valid[None, :, None, None, None, :], scores, NEG)
    sink = jnp.broadcast_to(sinks.astype(jnp.float32).reshape(1, 1, N_KV_HEADS, Q_PER_KV, 1, 1),
                            scores.shape[:-1] + (1,))
    p = jax.nn.softmax(jnp.concatenate([scores, sink], axis=-1), axis=-1)[..., :WINDOW]
    o = jnp.einsum('bnkgqj,bnjkd->bnqkgd', p.astype(v.dtype), vb)
    return o.reshape(B, S, BRANCH_W)

def multiscale_pool(xc, w_map, scale):
    B, S, _ = xc.shape
    xg = xc.reshape(B, S, POOL_GROUPS, POOL_GW).astype(jnp.float32)
    cs = jnp.pad(jnp.cumsum(xg, axis=1), ((0, 0), (1, 0), (0, 0), (0, 0)))
    t = jnp.arange(S)
    outs = []
    for g, w in enumerate(POOL_WINDOWS):
        upper = cs[:, 1:, g]
        lower = jnp.pad(cs[:, :S + 1 - w, g], ((0, 0), (w - 1, 0), (0, 0)))
        cnt = jnp.minimum(t + 1, w).astype(jnp.float32)[None, :, None]
        outs.append((upper - lower) / cnt - xg[:, :, g])
    pooled = jnp.stack(outs, axis=2).astype(xc.dtype)
    y = jnp.einsum('bsgc,gcd->bsgd', pooled, w_map).reshape(B, S, D_MODEL)
    return y * scale

def conformer_conv(zd, w_dw, b_dw, ln_g, ln_b, w_pw):
    a, gate = zd[..., :BRANCH_W], zd[..., BRANCH_W:]
    y = a * jax.nn.sigmoid(gate)
    y = lax.conv_general_dilated(y, w_dw[:, None, :], window_strides=(1,),
                                 padding=[(CONV_W - 1, 0)],
                                 dimension_numbers=('NWC', 'WIO', 'NWC'),
                                 feature_group_count=BRANCH_W) + b_dw
    y = jax.nn.silu(layer_norm(y, ln_g, ln_b))
    return y @ w_pw

def setup_inputs(seed: int = 0) -> dict:
    key = jax.random.key(seed)
    ks = jax.random.split(key, 32)
    L, D = DEPTH, D_MODEL

    def nrm(k, shape, scale):
        return jax.random.normal(k, shape, jnp.float32) * scale

    def gain(k, shape):
        return 1.0 + nrm(k, shape, 0.05)

    return {
        "x": nrm(ks[0], (BATCH, SEQ, D), 1.0),
        "norm_mix_pre": gain(ks[1], (L, D)),
        "norm_mix_post": gain(ks[2], (L, D)),
        "norm_ffn_pre": gain(ks[3], (L, D)),
        "norm_ffn_post": gain(ks[4], (L, D)),
        "w_in": nrm(ks[5], (L, D, D_IN), D ** -0.5),
        "a_vnorm_g": gain(ks[6], (L, BRANCH_W)),
        "a_vnorm_b": nrm(ks[7], (L, BRANCH_W), 0.02),
        "a_w_s": nrm(ks[8], (L, GMLP_GROUPS, GMLP_BLOCK, GMLP_BLOCK), GMLP_BLOCK ** -0.5),
        "a_b_s": gain(ks[9], (L, GMLP_GROUPS, GMLP_BLOCK)),
        "a_w_out": nrm(ks[10], (L, BRANCH_W, D), BRANCH_W ** -0.5),
        "b_sinks": nrm(ks[11], (L, N_Q_HEADS), 0.5),
        "b_w_out": nrm(ks[12], (L, BRANCH_W, D), BRANCH_W ** -0.5),
        "c_w_map": nrm(ks[13], (L, POOL_GROUPS, POOL_GW, POOL_OUT_GW), POOL_GW ** -0.5),
        "c_scale": gain(ks[14], (L, D)),
        "d_w_dw": nrm(ks[15], (L, CONV_W, BRANCH_W), CONV_W ** -0.5),
        "d_b_dw": nrm(ks[16], (L, BRANCH_W), 0.02),
        "d_ln_g": gain(ks[17], (L, BRANCH_W)),
        "d_ln_b": nrm(ks[18], (L, BRANCH_W), 0.02),
        "d_w_out": nrm(ks[19], (L, BRANCH_W, D), BRANCH_W ** -0.5),
        "w_gate": nrm(ks[20], (L, N_BRANCH, D, D), D ** -0.5),
        "b_gate": nrm(ks[21], (L, N_BRANCH, D), 0.02),
        "w_o": nrm(ks[22], (L, D, D), D ** -0.5),
        "w_ffn_in": nrm(ks[23], (L, D, 2 * D_FF), D ** -0.5),
        "w_ffn_out": nrm(ks[24], (L, D_FF, D), D_FF ** -0.5),
    }

def reference(x, norm_mix_pre, norm_mix_post, norm_ffn_pre, norm_ffn_post, w_in,
              a_vnorm_g, a_vnorm_b, a_w_s, a_b_s, a_w_out, b_sinks, b_w_out,
              c_w_map, c_scale, d_w_dw, d_b_dw, d_ln_g, d_ln_b, d_w_out,
              w_gate, b_gate, w_o, w_ffn_in, w_ffn_out):
    o_b = IN_A
    o_c = o_b + IN_B
    o_d = o_c + IN_C
    for l in range(DEPTH):
        h = rms_norm(x, norm_mix_pre[l])
        z = h @ w_in[l]
        za, zb, zc, zd = z[..., :o_b], z[..., o_b:o_c], z[..., o_c:o_d], z[..., o_d:]
        q = zb[..., :IN_B_Q]
        k = zb[..., IN_B_Q:IN_B_Q + IN_B_KV]
        v = zb[..., IN_B_Q + IN_B_KV:]
        y_a = gmlp_mixer(za, a_vnorm_g[l], a_vnorm_b[l], a_w_s[l], a_b_s[l]) @ a_w_out[l]
        y_b = sliding_window_attention(q, k, v, b_sinks[l]) @ b_w_out[l]
        y_c = multiscale_pool(zc, c_w_map[l], c_scale[l])
        y_d = conformer_conv(zd, d_w_dw[l], d_b_dw[l], d_ln_g[l], d_ln_b[l], d_w_out[l])
        merged = jax.nn.sigmoid(h @ w_gate[l, 0] + b_gate[l, 0]) * y_a
        merged = merged + jax.nn.sigmoid(h @ w_gate[l, 1] + b_gate[l, 1]) * y_b
        merged = merged + jax.nn.sigmoid(h @ w_gate[l, 2] + b_gate[l, 2]) * y_c
        merged = merged + jax.nn.sigmoid(h @ w_gate[l, 3] + b_gate[l, 3]) * y_d
        x = x + rms_norm(merged @ w_o[l], norm_mix_post[l])
        h2 = rms_norm(x, norm_ffn_pre[l])
        gu = h2 @ w_ffn_in[l]
        f = (jax.nn.silu(gu[..., :D_FF]) * gu[..., D_FF:]) @ w_ffn_out[l]
        x = x + rms_norm(f, norm_ffn_post[l])
    return x


_drawn_inputs = setup_inputs


def setup_inputs(seed=0):
    import zlib

    import numpy as np

    out = dict(_drawn_inputs(seed))
    spreads = {}
    factors = {'a_vnorm_g': 3.343,
     'a_vnorm_b': 8.0,
     'a_b_s': 3.03,
     'b_sinks': 8.0,
     'd_b_dw': 3.766,
     'd_ln_g': 2.732,
     'd_ln_b': 8.0,
     'b_gate': 8.0}
    for name, (base, spread) in spreads.items():
        noise = np.random.default_rng([zlib.crc32(name.encode()), seed]).standard_normal(out[name].shape)
        drawn = base * np.exp(spread * noise) if base else spread * noise
        out[name] = __import__('jax').numpy.asarray(drawn.astype(out[name].dtype))
    for name, factor in factors.items():
        out[name] = (out[name] * factor).astype(out[name].dtype)
    return out
```

```python
from contextlib import ExitStack

import numpy as np

import concourse.bass as bass
from concourse import mybir

F32 = mybir.dt.float32
F16 = mybir.dt.float16
I32 = mybir.dt.int32
ALU = mybir.AluOpType
ACT = mybir.ActivationFunctionType
AX = mybir.AxisListType

P = 128
D = 2048
S = 512
KT = D // P
BW = 512
BT = BW // P
NB = S // P
DFF = 5632
FT = DFF // P
HD = 64
CONV_W = 31
POOL_WINDOWS = (2, 4, 8, 16)
CHUNK = 64
RMS_EPS, LN_EPS = 1e-6, 1e-5
MASKED = -1e30
WSCALE = 256.0
UNSCALE = 1.0 / WSCALE

CW = KT * 2 * P
BRW = (3 * BT + 1) * 2 * P
OK = 11
OC = FT // OK
OW = OK * 2 * P
N_IN = 13
PAIRS = KT // 2
C_D, C_B, C_AV, C_AU, C_C = 0, 4, 7, 9, 11
C_G = N_IN
C_O = C_G + 5 * PAIRS
C_F = C_O + PAIRS
C_X = C_F + FT
C_END = C_X + OC * PAIRS

E_G = N_IN
E_O = E_G + 4 * PAIRS
E_F = E_O + PAIRS
E_X = E_F + FT

V_PRE, V_POST, V_FPRE, V_FPOST, V_CS = 0, KT, 2 * KT, 3 * KT, 4 * KT
V_BG = 5 * KT
V_DW = V_BG + 4 * KT
V_DB = V_DW + CONV_W * BT
V_LG = V_DB + BT
V_LB = V_LG + BT
NV = V_LB + BT
R_VG, R_VB, R_BS, R_SK = 0, BW, 2 * BW, 3 * BW
NR = 3 * BW + 8

HALF0, HALF1 = slice(0, 64), slice(64, 128)


class Count:

    def __init__(self):
        self.n, self.turn, self.per_turn = 0, None, 0

    def up(self):
        self.n += 1
        return self.now()

    def now(self):
        return self.n if self.turn is None else self.turn * self.per_turn + self.n

    def enter(self, turn, per_turn):
        self.turn, self.per_turn, self.start = turn, per_turn, self.n

    def leave(self, turns):
        assert self.n - self.start == self.per_turn, (self.n, self.start)
        self.n, self.turn = self.start + self.per_turn * turns, None


def at(base, per_turn=0, turn=None):
    return base if turn is None else turn * per_turn + base


def block_program(nc, x, w_in, w_gate, w_branch, w_o, w_ffn_in, w_ffn_out, vecs_d, rows_d, ws_d,
                  out, x2_spill):
    with ExitStack() as ctx:
        def sb(name, shape, dt):
            return ctx.enter_context(nc.sbuf_tensor(name, shape, dt))

        def sem(name):
            return ctx.enter_context(nc.semaphore(name))

        stage = sb("stage", [P, 2, CW], F32)
        whi = sb("whi", [P, 2, CW], F16)
        wlo = sb("wlo", [P, 2, CW], F16)
        region_a = sb("region_a", [P, FT * S], F32)
        region_b = sb("region_b", [P, KT * S], F32)
        work = sb("work", [P, 4, S], F32)
        vecs = sb("vecs", [P, NV], F32)
        rows = sb("rows", [P, NR], F32)
        wst = sb("wst", [P, BT, P], F32)
        ident = sb("ident", [P, P], F32)
        ones = sb("ones", [P, P], F32)
        mask = sb("mask", [P, 2 * P], F32)
        rinv = sb("rinv", [P, S], F32)
        std = sb("std", [P, S], F32)
        lnstat = sb("lnstat", [P, NB, 6], F32)
        lnmv = sb("lnmv", [P, NB, 2], F32)
        lnrs = sb("lnrs", [P, NB], F32)
        smax = sb("smax", [P, 4, 4], F32)
        poolfix = sb("poolfix", [P, 4, 16], F32)
        posi = sb("posi", [P, 16], I32)

        def view(region, start, n, dt, pattern=None, **sizes):
            v = region[:, start:start + n]
            if dt != F32:
                v = v.bitcast(dt)
            return v.rearrange(pattern, **sizes) if pattern else v

        K2 = KT * S
        h = view(region_a, 0, K2, F16, "p (k l s) -> p k l s", k=KT, l=2)
        b2 = BT * S
        a_out, b_out, c_out, d_out = (
            view(region_a, K2 + i * b2, b2, F16, "p (k l s) -> p k l s", k=BT, l=2) for i in range(4))
        a_v = view(region_a, K2, b2, F32, "p (k s) -> p k s", k=BT)
        key = view(region_a, K2 + 2 * b2, S, F32)
        val = view(region_a, K2 + 2 * b2 + S, S, F32)
        val_tok = view(region_a, K2 + 2 * b2 + 2 * S, S, F32, "p (m d) -> p m d", m=NB)
        glu = view(region_a, K2 + 3 * b2, b2, F32, "p (k s) -> p k s", k=BT)
        gate_at = K2 + 4 * b2
        gates = view(region_a, gate_at, 8 * S, F32, "p (b t s) -> p b t s", b=4, t=2)
        query = view(region_a, gate_at, b2, F32, "p (k s) -> p k s", k=BT)
        prob = view(region_a, gate_at + b2, b2, F32, "p (u k j) -> p u k j", u=2, k=4)
        c_x = view(region_a, gate_at + 8 * S, b2, F32, "p (k s) -> p k s", k=BT)
        mix = view(region_a, 0, K2, F32, "p (k s) -> p k s", k=KT)
        res = view(region_a, K2, K2, F32, "p (k s) -> p k s", k=KT)
        f = view(region_a, 0, FT * S, F16, "p (k l s) -> p k l s", k=FT, l=2)
        x_in = view(region_b, 0, K2, F32, "p (k s) -> p k s", k=KT)
        conv = view(region_b, 0, b2, F32, "p (k s) -> p k s", k=BT)
        prob_t = view(region_b, b2, b2, F32, "p (u m q) -> p u m q", u=2, m=2)
        a_vn = view(region_b, 2 * b2, b2, F32, "p (m c) -> p m c", m=NB)
        a_u = view(region_b, 3 * b2, b2, F32, "p (k s) -> p k s", k=BT)
        merged = view(region_b, 0, K2, F16, "p (k l s) -> p k l s", k=KT, l=2)
        h2 = merged
        ffn = x_in
        x2_back = stage[:, :, :].rearrange("p u (k s) -> p (u k) s", s=S)

        psum = ctx.enter_context(nc.psum_tensor("psum", [P, 8, S], F32))

        x_landed = [sem(f"x_landed{i}") for i in range(4)]
        vecs_landed, rows_landed, ws_landed = sem("vecs_landed"), sem("rows_landed"), sem("ws_landed")
        w_landed = [sem(f"w_landed{i}") for i in range(2)]
        res_landed = [sem(f"res_landed{i}") for i in range(2)]
        x2_spilled, x2_landed = sem("x2_spilled"), [sem(f"x2_landed{i}") for i in range(2)]
        out_stored = sem("out_stored")
        consts_ready, ident_zero, ident_ready, posi_ready = (
            sem("consts_ready"), sem("ident_zero"), sem("ident_ready"), sem("posi_ready"))
        cs_ready, wst_masked = sem("cs_ready"), sem("wst_masked")
        hi_ready, lo_ready = sem("hi_ready"), sem("lo_ready")
        tile0_done = sem("tile0_done")
        chunk_done = sem("chunk_done")
        evicted0, evicted1 = sem("evicted0"), sem("evicted1")
        sq_ready, sq_used = sem("sq_ready"), sem("sq_used")
        sum_ready, std_ready, rinv_ready = sem("sum_ready"), sem("std_ready"), sem("rinv_ready")
        xr_ready, h_hi, h_lo = sem("xr_ready"), sem("h_hi"), sem("h_lo")
        glu_ready = sem("glu_ready")
        conv_done, mean_done, centered, csq_ready, var_done, cstd_ready, cnorm_ready, silu_ready, d_hi, d_lo = (
            sem(n) for n in ("conv_done", "mean_done", "centered", "csq_ready", "var_done",
                             "cstd_ready", "cnorm_ready", "silu_ready", "d_hi", "d_lo"))
        vt_done, vt_ready, s_done, s_used, s_shift, exp_ready, prob_ready, pt_done, pt_ready = (
            sem(n) for n in ("vt_done", "vt_ready", "s_done", "s_used", "s_shift", "exp_ready",
                             "prob_ready", "pt_done", "pt_ready"))
        pv_done, b_hi, b_lo = sem("pv_done"), sem("b_hi"), sem("b_lo")
        av_done, av_used, lnvar_ready, lnstd_ready, vn_ready, sv_done, au_ready, a_hi, a_lo = (
            sem(n) for n in ("av_done", "av_used", "lnvar_ready", "lnstd_ready", "vn_ready",
                             "sv_done", "au_ready", "a_hi", "a_lo"))
        win_ready, win_used, c_hi, c_lo = (
            sem(n) for n in ("win_ready", "win_used", "c_hi", "c_lo"))
        y_ready, y_used, merged_ready, m_hi, m_lo = (
            sem(n) for n in ("y_ready", "y_used", "merged_ready", "m_hi", "m_lo"))
        osq_ready, osq_used, osum_ready = sem("osq_ready"), sem("osq_used"), sem("osum_ready")
        x2_ready, x2sq_ready, f_ready, f_hi, f_lo, y_out = (
            sem(n) for n in ("x2_ready", "x2sq_ready", "f_ready", "f_hi", "f_lo", "y_out"))
        act_step, dve_step, pool_step = sem("act_step"), sem("dve_step"), sem("pool_step")

        block = ctx.enter_context(nc.Block())

        @block.sync
        def _(sp):
            def load(n0, src, width=CW, per_turn=0, turn=None):
                if n0 >= 2:
                    sp.wait_ge(lo_ready, at(n0 - 1, per_turn, turn))
                sp.dma_start(stage[:, n0 % 2, 0:width], src).then_inc(w_landed[n0 % 2], 16)

            def pair_stage(n0, jj, per_turn=0, turn=None):
                j = at(jj, 2, turn)
                for b in range(4):
                    src = w_gate[jj, b] if turn is None else \
                        w_gate[bass.ds(j, 1), b].rearrange("o p n -> (o p) n")
                    load(n0 + b, src, CW, per_turn, turn)
                src = w_branch[jj] if turn is None else \
                    w_branch[bass.ds(j, 1)].rearrange("o p n -> (o p) n")
                load(n0 + 4, src, BRW, per_turn, turn)

            def one(w, i):
                return w[bass.ds(i, 1)].rearrange("o p n -> (o p) n")

            sp.dma_start(vecs[:, :], vecs_d).then_inc(vecs_landed, 16)
            for i in range(4):
                sp.dma_start(x_in[:, 4 * i:4 * i + 4, :], x[:, 4 * i:4 * i + 4, :]).then_inc(x_landed[i], 16)
            load(0, w_in[0])
            load(1, w_in[1])
            sp.dma_start(rows[:, :], rows_d.partition_broadcast(P)).then_inc(rows_landed, 16)
            sp.dma_start(wst[:, :, :], ws_d).then_inc(ws_landed, 16)
            for n in range(2, N_IN):
                load(n, w_in[n])
            pair_stage(C_G, 0)
            with sp.Fori(0, 3) as turn:
                pair_stage(C_G + 5, 1, 10, turn)
                pair_stage(C_G + 10, 2, 10, turn)
            pair_stage(C_G + 35, 7)
            load(C_O, w_o[0])
            load(C_O + 1, w_o[1])
            sp.wait_ge(chunk_done, C_O)
            for i in range(2):
                sp.dma_start(res[:, 8 * i:8 * i + 8, :], x[:, 8 * i:8 * i + 8, :]).then_inc(res_landed[i], 16)
            with sp.Fori(0, PAIRS // 2 - 1) as turn:
                for t in range(2):
                    load(C_O + 2 + t, one(w_o, at(2 + t, 2, turn)), CW, 2, turn)
            load(C_F, w_ffn_in[0])
            load(C_F + 1, w_ffn_in[1])
            for i in range(4):
                sp.wait_ge(x2_ready, 4 * i + 4)
                sp.dma_start(x2_spill[:, 4 * i:4 * i + 4, :], res[:, 4 * i:4 * i + 4, :]).then_inc(x2_spilled, 16)
            with sp.Fori(0, FT // 2 - 1) as turn:
                for t in range(2):
                    load(C_F + 2 + t, one(w_ffn_in, at(2 + t, 2, turn)), CW, 2, turn)
            with sp.Fori(0, PAIRS) as turn:
                for c in range(OC):
                    load(C_X + c, one(w_ffn_out, at(c, OC, turn)), OW, OC, turn)
            sp.wait_ge(x2_spilled, 64)
            for i in (1, 0):
                sp.wait_ge(lo_ready, C_END - i)
                sp.dma_start(x2_back[:, 8 * i:8 * i + 8, :], x2_spill[:, 8 * i:8 * i + 8, :]).then_inc(x2_landed[i], 16)
            for i in range(PAIRS):
                sp.wait_ge(y_out, 2 * i + 2)
                sp.dma_start(out[:, 2 * i:2 * i + 2, :], x2_back[:, 2 * i:2 * i + 2, :]).then_inc(out_stored, 16)
            sp.wait_ge(out_stored, 16 * PAIRS)

        @block.gpsimd
        def _(pool):
            step = Count()
            nc.gpsimd.memset(ones[:, :], 1.0).then_inc(consts_ready, 1)
            nc.gpsimd.memset(ident[:, :], 0.0).then_inc(ident_zero, 1)
            nc.gpsimd.memset(mask[:, :], 0.0).then_inc(pool_step, 1)
            pool.wait_ge(pool_step, step.up())
            nc.gpsimd.memset(mask[HALF0, 0:CHUNK], MASKED).then_inc(consts_ready, 1)
            nc.gpsimd.memset(mask[HALF0, 3 * CHUNK:4 * CHUNK], MASKED).then_inc(consts_ready, 1)
            pool.wait_ge(consts_ready, 3)
            nc.gpsimd.memset(mask[HALF1, 0:2 * CHUNK], MASKED).then_inc(consts_ready, 1)
            pool.wait_ge(consts_ready, 4)
            pool.wait_ge(ident_zero, 1)
            nc.gpsimd.affine_select(out=ident[:, :], in_=ident[:, :], compare_op=ALU.not_equal, fill=1.0,
                                    base=0, pattern=[[-1, P]], channel_multiplier=1).then_inc(ident_ready, 1)
            nc.gpsimd.iota(posi[:, :], [[1, 16]], base=1, channel_multiplier=0).then_inc(posi_ready, 1)
            pool.wait_ge(ws_landed, 16)
            pool.wait_ge(ident_ready, 1)
            pool.wait_ge(posi_ready, 1)
            nc.gpsimd.memset(wst[HALF1, :, 0:CHUNK], 0.0).then_inc(wst_masked, 1)
            pool.wait_ge(wst_masked, 1)

            for i in range(BT):
                pool.wait_ge(evicted1, i + 1)
                nc.gpsimd.tensor_tensor(glu[:, i, :], work[:, 2 * (i % 2), :], work[:, 2 * (i % 2) + 1, :],
                                        ALU.mult).then_inc(glu_ready, 1)

            pool.wait_ge(evicted1, C_C + 2)
            for g in range(BT):
                if g >= 2:
                    pool.wait_ge(win_used, g - 1)
                src = c_x[:, g, :]
                for k in range(g + 1):
                    d = 1 << k
                    dst = work[:, 2 * (g % 2) + (g - k) % 2, :]
                    nc.gpsimd.tensor_copy(dst[:, 0:d], src[:, 0:d]).then_inc(pool_step, 1)
                    step.up()
                    last = nc.gpsimd.tensor_tensor(dst[:, d:S], src[:, d:S], src[:, 0:S - d], ALU.add)
                    last.then_inc(pool_step, 1)
                    pool.wait_ge(pool_step, step.up())
                    src = dst
                pool.wait_ge(posi_ready, 2)
                nc.gpsimd.tensor_tensor(src[:, 0:16], src[:, 0:16], poolfix[:, g, :], ALU.mult).then_inc(win_ready, 1)

            for phase in range(2):
                if phase == 0:
                    pool.wait_ge(m_lo, KT)
                else:
                    pool.wait_ge(h_lo, 2 * KT)
                nc.gpsimd.memset(std[:, :], 0.0).then_inc(pool_step, 1)
                pool.wait_ge(pool_step, step.up())
                with pool.Fori(0, PAIRS) as turn:
                    step.enter(turn, 1)
                    for t in range(2):
                        pool.wait_ge(osq_ready, at(2 * PAIRS * phase + t + 1, 2, turn))
                        if t == 1:
                            pool.wait_ge(pool_step, step.up())
                        ins = nc.gpsimd.tensor_tensor(std[:, :], std[:, :], work[:, t, :], ALU.add)
                        ins.then_inc(pool_step if t == 0 else osq_used, 1)
                    pool.wait_ge(osq_used, at(PAIRS * phase + 1, 1, turn))
                step.leave(PAIRS)

        @block.scalar
        def _(act):
            step = Count()

            def hi(n0, width=CW, per_turn=0, turn=None):
                act.wait_ge(w_landed[n0 % 2], at(16 * (n0 // 2 + 1), 8 * per_turn, turn))
                if n0 >= 2:
                    act.wait_ge(chunk_done, at(n0 - 1, per_turn, turn))
                nc.scalar.activation(whi[:, n0 % 2, 0:width], stage[:, n0 % 2, 0:width], ACT.Copy,
                                     scale=WSCALE).then_inc(hi_ready, 1)

            def evict0(e0, dst, func=ACT.Identity, per_turn=0, turn=None, **kw):
                act.wait_ge(tile0_done, at(e0 + 1, per_turn, turn))
                nc.scalar.activation(dst, psum[:, 0, :], func, scale=UNSCALE, **kw).then_inc(evicted0, 1)

            def evict1(n0, dst, func=ACT.Identity, per_turn=0, turn=None, **kw):
                act.wait_ge(chunk_done, at(n0 + 1, per_turn, turn))
                nc.scalar.activation(dst, psum[:, 1, :], func, scale=UNSCALE, **kw).then_inc(evicted1, 1)

            def mean_root(src, n, eps, done, value, ready):
                act.wait_ge(done, value)
                nc.scalar.activation(std[:, :], src, ACT.Sqrt, scale=1.0 / n, bias=eps).then_inc(ready, 1)

            for b in range(PAIRS):
                if b % 2 == 0:
                    act.wait_ge(x_landed[b // 2], 16)
                if b >= 2:
                    act.wait_ge(sq_used, b - 1)
                nc.scalar.activation(work[:, 2 * (b % 2):2 * (b % 2) + 2, :], x_in[:, 2 * b:2 * b + 2, :],
                                     ACT.Square).then_inc(sq_ready, 1)
            mean_root(psum[:, 7, :], D, RMS_EPS, sum_ready, 1, std_ready)
            hi(0)

            def h_high(dst, vec, phase):
                for k in range(KT):
                    act.wait_ge(xr_ready, PAIRS * phase + k // 2 + 1)
                    nc.scalar.activation(dst[:, k, 0, :], work[:, k % 4, :], ACT.Copy,
                                         scale=vecs[:, vec + k:vec + k + 1]).then_inc(h_hi, 1)

            h_high(h, V_PRE, 0)

            def exp_part(u):
                act.wait_ge(s_shift, u + 1)
                lo_key = 0 if u >= 2 else P
                nc.scalar.activation(prob[:, u % 2, :, lo_key:], prob[:, u % 2, :, lo_key:], ACT.Exp).then_inc(exp_ready, 1)
                nc.scalar.activation(smax[:, 1, :], smax[:, 1, :], ACT.Exp).then_inc(exp_ready, 1)

            def evict_prob_t(u):
                act.wait_ge(pt_done, u + 1)
                if u >= 2:
                    act.wait_ge(pv_done, u - 1)
                m0 = 0 if u >= 2 else 1
                nc.scalar.activation(prob_t[:, u % 2, m0:, :], psum[:, 4 + m0:6, :], ACT.Copy).then_inc(pt_ready, 1)

            def heads_high(u):
                m, g = u // 2, u % 2
                half = HALF1 if g else HALF0
                act.wait_ge(pv_done, u + 1)
                nc.scalar.activation(b_out[half, :, 0, m * P:m * P + P],
                                     psum[half, 6, :].rearrange("p (k q) -> p k q", k=4), ACT.Copy).then_inc(b_hi, 1)

            def tasks(k):
                if k == 16:
                    act.wait_ge(centered, 1)
                    nc.scalar.activation(work[:, :, :], conv[:, :, :], ACT.Square).then_inc(csq_ready, 1)
                if k == 15:
                    act.wait_ge(vt_done, 1)
                    nc.scalar.activation(val_tok[:, :, :], psum[:, 7, :].rearrange("p (m d) -> p m d", m=NB),
                                         ACT.Copy).then_inc(vt_ready, 1)
                if k == 17:
                    mean_root(psum[:, 6, :], BW, LN_EPS, var_done, 1, cstd_ready)
                if k == 18:
                    act.wait_ge(cnorm_ready, 1)
                    for i in range(BT):
                        nc.scalar.activation(conv[:, i, :], conv[:, i, :], ACT.Silu,
                                             scale=vecs[:, V_LG + i:V_LG + i + 1],
                                             bias=vecs[:, V_LB + i:V_LB + i + 1]).then_inc(silu_ready, 1)
                    act.wait_ge(silu_ready, BT)
                    nc.scalar.activation(d_out[:, :, 0, :], conv[:, :, :], ACT.Copy).then_inc(d_hi, 1)
                if 0 <= k - 17 < 8:
                    evict_prob_t(k - 17)
                if 0 <= k - 18 < 8:
                    heads_high(k - 18)
                if 0 <= k - 15 < 8:
                    exp_part(k - 15)
                if k == 23:
                    act.wait_ge(lnvar_ready, NB)
                    nc.scalar.activation(lnrs[:, :], lnmv[:, :, 1], ACT.Sqrt, bias=LN_EPS).then_inc(lnstd_ready, 1)
                if k == 28:
                    act.wait_ge(au_ready, BT)
                    nc.scalar.activation(a_out[:, :, 0, :], a_u[:, :, :], ACT.Copy).then_inc(a_hi, 1)
                if k == 31:
                    act.wait_ge(win_used, BT)
                    nc.scalar.activation(c_out[:, :, 0, :], c_x[:, :, :], ACT.Copy).then_inc(c_hi, 1)

            def evictions(n):
                if n < C_B:
                    if n >= 2:
                        act.wait_ge(glu_ready, n - 1)
                    return [(work[:, 2 * (n % 2), :], ACT.Identity), (work[:, 2 * (n % 2) + 1, :], ACT.Sigmoid)]
                if n < C_B + 2:
                    return [(query[:, 2 * (n - C_B) + t, :], ACT.Identity) for t in range(2)]
                if n == C_B + 2:
                    return [(key, ACT.Identity), (val, ACT.Identity)]
                if n < C_C:
                    dst, i = (a_v, n - C_AV) if n < C_AU else (a_u, n - C_AU)
                    return [(dst[:, 2 * i + t, :], ACT.Gelu) for t in range(2)]
                return [(c_x[:, 2 * (n - C_C) + t, :], ACT.Identity) for t in range(2)]

            for n in range(N_IN):
                hi(n + 1)
                tasks(2 * n)
                to = evictions(n)
                evict0(n, *to[0])
                tasks(2 * n + 1)
                evict1(n, *to[1])

            def pair_stage(n0, e0, jj, task=None, per_turn=0, turn=None, next_width=CW):
                ept = 8 if turn is not None else 0
                for b in range(4):
                    hi(n0 + b + 1, BRW if b == 3 else CW, per_turn, turn)
                    if task:
                        tasks(2 * (n0 + b))
                    if b == 0 and jj >= 1:
                        act.wait_ge(y_used, at(8 * jj, 16, turn))
                    for t, ev in ((0, evict0), (1, evict1)):
                        col = V_BG + b * KT + 2 * jj + t
                        bias = vecs[:, col:col + 1] if turn is None else vecs[:, bass.ds(at(col, 4, turn), 1)]
                        if t == 0:
                            evict0(e0 + b, gates[:, b, 0, :], ACT.Sigmoid, ept, turn, bias=bias)
                            if task:
                                tasks(2 * (n0 + b) + 1)
                        else:
                            evict1(n0 + b, gates[:, b, 1, :], ACT.Sigmoid, per_turn, turn, bias=bias)
                hi(n0 + 5, next_width, per_turn, turn)
                for t in range(2):
                    act.wait_ge(merged_ready, at(2 * jj + t + 1, 4, turn))
                    j = 2 * jj + t
                    dst = merged[:, j, 0, :] if turn is None else \
                        merged[:, bass.ds(at(j, 4, turn), 1), 0, :].rearrange("p o s -> p (o s)")
                    nc.scalar.activation(dst, work[:, 2 * t, :], ACT.Copy).then_inc(m_hi, 1)

            pair_stage(C_G, E_G, 0, task=True)
            with act.Fori(0, 3) as turn:
                pair_stage(C_G + 5, E_G + 4, 1, None, 10, turn)
                pair_stage(C_G + 10, E_G + 8, 2, None, 10, turn)
            pair_stage(C_G + 35, E_G + 28, 7)

            def norm_pair(n0, e0, dst, j0, phase, pairs_before, pairs_per_turn, per_turn, turn):
                for t in range(2):
                    if t == 0:
                        act.wait_ge(tile0_done, at(e0 + 1, pairs_per_turn, turn))
                        if pairs_before > 0:
                            act.wait_ge(osq_used, at(PAIRS * phase + pairs_before, pairs_per_turn, turn))
                    else:
                        act.wait_ge(chunk_done, at(n0 + 1, per_turn, turn))
                    nc.scalar.activation(work[:, t, :], psum[:, t, :], ACT.Square, scale=UNSCALE).then_inc(osq_ready, 1)
                    j = at(j0 + t, 2 * pairs_per_turn, turn)
                    d = dst[:, j, :] if turn is None else dst[:, bass.ds(j, 1), :].rearrange("p o s -> p (o s)")
                    nc.scalar.activation(d, psum[:, t, :], ACT.Identity, scale=UNSCALE).then_inc(evicted1 if t else evicted0, 1)

            def o_chunk(n0, e0, j0, pairs_before, turn):
                hi(n0 + 1, CW, 2, turn)
                norm_pair(n0, e0, mix, j0, 0, pairs_before, 2, 2, turn)

            o_chunk(C_O, E_O, 0, 0, None)
            o_chunk(C_O + 1, E_O + 1, 2, 1, None)
            with act.Fori(0, PAIRS // 2 - 1) as turn:
                o_chunk(C_O + 2, E_O + 2, 4, 2, turn)
                o_chunk(C_O + 3, E_O + 3, 6, 3, turn)

            mean_root(psum[:, 7, :], D, RMS_EPS, osum_ready, 1, std_ready)
            for b in range(PAIRS):
                act.wait_ge(x2_ready, 2 * b + 2)
                if b >= 2:
                    act.wait_ge(sq_used, PAIRS - 1 + b - 1)
                nc.scalar.activation(work[:, 2 * (b % 2):2 * (b % 2) + 2, :], res[:, 2 * b:2 * b + 2, :],
                                     ACT.Square).then_inc(sq_ready, 1)
            mean_root(psum[:, 7, :], D, RMS_EPS, sum_ready, 2, std_ready)
            h_high(h2, V_FPRE, 1)

            def ffn_chunk(n0, e0, j0, width, turn):
                hi(n0 + 1, width, 2, turn)
                w = 2 * ((n0 - C_F) % 2)
                if n0 >= C_F + 2:
                    act.wait_ge(f_lo, at(j0 - 1, 2, turn))
                else:
                    act.wait_ge(h_lo, 2 * KT)
                evict0(e0, work[:, w, :], ACT.Silu, 2, turn)
                evict1(n0, work[:, w + 1, :], ACT.Identity, 2, turn)
                act.wait_ge(f_ready, at(j0 + 1, 2, turn))
                j = at(j0, 2, turn)
                dst = f[:, j, 0, :] if turn is None else \
                    f[:, bass.ds(j, 1), 0, :].rearrange("p o s -> p (o s)")
                nc.scalar.activation(dst, work[:, w, :], ACT.Copy).then_inc(f_hi, 1)

            ffn_chunk(C_F, E_F, 0, CW, None)
            ffn_chunk(C_F + 1, E_F + 1, 1, CW, None)
            with act.Fori(0, FT // 2 - 2) as turn:
                ffn_chunk(C_F + 2, E_F + 2, 2, CW, turn)
                ffn_chunk(C_F + 3, E_F + 3, 3, CW, turn)
            ffn_chunk(C_X - 2, E_X - 2, FT - 2, CW, None)
            ffn_chunk(C_X - 1, E_X - 1, FT - 1, OW, None)

            def out_pair(n0, e0, j0, pairs_before, last, turn):
                for c in range(OC):
                    if not (last and c == OC - 1):
                        hi(n0 + c + 1, OW, OC, turn)
                if pairs_before == 0:
                    act.wait_ge(f_lo, FT)
                norm_pair(n0 + OC - 1, e0, ffn, j0, 1, pairs_before, 1, OC, turn)

            out_pair(C_X, E_X, 0, 0, False, None)
            with act.Fori(0, PAIRS - 2) as turn:
                out_pair(C_X + OC, E_X + 1, 2, 1, False, turn)
            out_pair(C_END - OC, E_X + PAIRS - 1, KT - 2, PAIRS - 1, True, None)
            mean_root(psum[:, 7, :], D, RMS_EPS, osum_ready, 2, std_ready)

        @block.vector
        def _(dve):
            step = Count()
            V = nc.vector

            def lo(n0, width=CW, per_turn=0, turn=None):
                dve.wait_ge(hi_ready, at(n0 + 1, per_turn, turn))
                V.scalar_tensor_tensor(out=wlo[:, n0 % 2, 0:width], in0=stage[:, n0 % 2, 0:width], scalar=WSCALE,
                                       in1=whi[:, n0 % 2, 0:width], op0=ALU.mult, op1=ALU.subtract).then_inc(lo_ready, 1)

            def inverse_root(value):
                dve.wait_ge(std_ready, value)
                V.reciprocal(rinv[:, :], std[:, :]).then_inc(rinv_ready, 1)
                dve.wait_ge(rinv_ready, value)

            def normed(src, dst, vec, phase):
                def scaled(b):
                    if b >= 2:
                        dve.wait_ge(h_lo, KT * phase + 2 * (b - 1))
                    V.tensor_tensor(work[:, 2 * (b % 2):2 * (b % 2) + 2, :], src[:, 2 * b:2 * b + 2, :],
                                    rinv[:, :].unsqueeze(1).to_broadcast([P, 2, S]), ALU.mult).then_inc(xr_ready, 1)
                scaled(0)
                for b in range(PAIRS):
                    if b + 1 < PAIRS:
                        scaled(b + 1)
                    dve.wait_ge(xr_ready, PAIRS * phase + b + 1)
                    for k in (2 * b, 2 * b + 1):
                        dve.wait_ge(h_hi, KT * phase + k + 1)
                        V.scalar_tensor_tensor(out=dst[:, k, 1, :], in0=work[:, k % 4, :],
                                               scalar=vecs[:, vec + k:vec + k + 1], in1=dst[:, k, 0, :],
                                               op0=ALU.mult, op1=ALU.subtract).then_inc(h_lo, 1)

            dve.wait_ge(vecs_landed, 16)
            V.tensor_scalar(vecs[:, V_CS:V_CS + KT], vecs[:, V_CS:V_CS + KT], UNSCALE, None, ALU.mult).then_inc(cs_ready, 1)
            dve.wait_ge(posi_ready, 1)
            for g, w in enumerate(POOL_WINDOWS):
                V.tensor_scalar(poolfix[:, g, :], posi[:, :], float(w), None, ALU.min).then_inc(dve_step, 1)
            for _ in range(4):
                step.up()
            dve.wait_ge(dve_step, step.now())
            V.reciprocal(poolfix[:, :, :], poolfix[:, :, :]).then_inc(dve_step, 1)
            dve.wait_ge(dve_step, step.up())
            for g, w in enumerate(POOL_WINDOWS):
                ins = V.tensor_scalar(poolfix[:, g, :], poolfix[:, g, :], float(w), None, ALU.mult)
                ins.then_inc(dve_step if g < 3 else posi_ready, 1)
                if g < 3:
                    step.up()
            lo(0)

            inverse_root(1)
            normed(x_in, h, V_PRE, 0)

            def softmax(u):
                m = u // 2
                k0 = 0 if m else P
                keys = 2 * P - k0
                pu = prob[:, u % 2, :, k0:]
                g = u % 2
                dve.wait_ge(s_done, u + 1)
                if u >= 2:
                    dve.wait_ge(pt_done, u - 1)
                bank = psum[:, 2:4, :].rearrange("p b (k j) -> p (b k) j", k=2)[:, :, k0:]
                V.scalar_tensor_tensor(out=pu, in0=bank, scalar=float(HD) ** -0.5,
                                       in1=mask[:, k0:].unsqueeze(1).to_broadcast([P, 4, keys]),
                                       op0=ALU.mult, op1=ALU.add).then_inc(s_used, 1)
                dve.wait_ge(s_used, u + 1)
                V.tensor_reduce(smax[:, 0, :], pu, AX.X, ALU.max).then_inc(dve_step, 1)
                dve.wait_ge(dve_step, step.up())
                sink = rows[:, R_SK + 4 * g:R_SK + 4 * g + 4]
                V.tensor_tensor(smax[:, 0, :], smax[:, 0, :], sink, ALU.max).then_inc(dve_step, 1)
                dve.wait_ge(dve_step, step.up())
                V.tensor_tensor(smax[:, 1, :], sink, smax[:, 0, :], ALU.subtract).then_inc(dve_step, 1)
                step.up()
                V.tensor_tensor(pu, pu, smax[:, 0, :].unsqueeze(2).to_broadcast([P, 4, keys]),
                                ALU.subtract).then_inc(s_shift, 1)
                dve.wait_ge(exp_ready, 2 * u + 2)
                V.tensor_reduce(smax[:, 2, :], pu, AX.X, ALU.add).then_inc(dve_step, 1)
                dve.wait_ge(dve_step, step.up())
                V.tensor_tensor(smax[:, 2, :], smax[:, 2, :], smax[:, 1, :], ALU.add).then_inc(dve_step, 1)
                dve.wait_ge(dve_step, step.up())
                if u >= 1:
                    dve.wait_ge(prob_ready, u)
                V.reciprocal(smax[:, 3, :], smax[:, 2, :]).then_inc(dve_step, 1)
                dve.wait_ge(dve_step, step.up())
                V.tensor_tensor(pu, pu, smax[:, 3, :].unsqueeze(2).to_broadcast([P, 4, keys]),
                                ALU.mult).then_inc(prob_ready, 1)

            def heads_low(u):
                m = u // 2
                half = HALF1 if u % 2 else HALF0
                dve.wait_ge(b_hi, u + 1)
                V.tensor_tensor(b_out[half, :, 1, m * P:m * P + P],
                                psum[half, 6, :].rearrange("p (k q) -> p k q", k=4),
                                b_out[half, :, 0, m * P:m * P + P], ALU.subtract).then_inc(b_lo, 1)

            def taps(first, last):
                for at_ in range(first, min(last, BT * CONV_W)):
                    i, q = at_ // CONV_W, at_ % CONV_W
                    tap = CONV_W - 1 - q
                    w = vecs[:, V_DW + tap * BT + i:V_DW + tap * BT + i + 1]
                    if q == 0:
                        dve.wait_ge(glu_ready, i + 1)
                        ins = V.tensor_scalar(conv[:, i, :], glu[:, i, :], w, vecs[:, V_DB + i:V_DB + i + 1],
                                              ALU.mult, ALU.add)
                    else:
                        ins = V.scalar_tensor_tensor(out=conv[:, i, q:S], in0=glu[:, i, 0:S - q], scalar=w,
                                                     in1=conv[:, i, q:S], op0=ALU.mult, op1=ALU.add)
                    if at_ == BT * CONV_W - 1:
                        ins.then_inc(conv_done, 1)
                    else:
                        ins.then_inc(dve_step, 1)
                        dve.wait_ge(dve_step, step.up())

            def value_stats(m):
                dve.wait_ge(av_done, m + 1)
                V.bn_stats(lnstat[:, m, :], psum[:, 7, :]).then_inc(dve_step, 1)
                dve.wait_ge(dve_step, step.up())
                V.bn_aggr(lnmv[:, m, :], lnstat[:, m, :]).then_inc(lnvar_ready, 1)
                dve.wait_ge(lnvar_ready, m + 1)
                V.tensor_scalar(a_vn[:, m, :], psum[:, 7, :], lnmv[:, m, 0:1], None, ALU.subtract).then_inc(av_used, 1)

            def tasks(k):
                if 2 <= k <= 13:
                    s = k // 2 - 1
                    taps(21 * s + (7 if k % 2 else 0), 21 * s + (21 if k % 2 else 7))
                if k == 15:
                    dve.wait_ge(mean_done, 1)
                    V.scalar_tensor_tensor(out=conv[:, :, :], in0=psum[:, 6, :].unsqueeze(1).to_broadcast([P, BT, S]),
                                           scalar=-1.0 / BW, in1=conv[:, :, :],
                                           op0=ALU.mult, op1=ALU.add).then_inc(centered, 1)
                if k == 17:
                    dve.wait_ge(cstd_ready, 1)
                    V.reciprocal(std[:, :], std[:, :]).then_inc(dve_step, 1)
                    dve.wait_ge(dve_step, step.up())
                    V.tensor_tensor(conv[:, :, :], conv[:, :, :], std[:, :].unsqueeze(1).to_broadcast([P, BT, S]),
                                    ALU.mult).then_inc(cnorm_ready, 1)
                if 0 <= k - 18 < 8:
                    heads_low(k - 18)
                if k == 15:
                    dve.wait_ge(rows_landed, 16)
                    dve.wait_ge(consts_ready, 4)
                if 0 <= k - 15 < 8:
                    softmax(k - 15)
                if k == 19:
                    dve.wait_ge(d_hi, 1)
                    V.tensor_tensor(d_out[:, :, 1, :], conv[:, :, :], d_out[:, :, 0, :], ALU.subtract).then_inc(d_lo, 1)
                if 0 <= k - 19 < NB:
                    value_stats(k - 19)
                if k == 24:
                    dve.wait_ge(lnstd_ready, 1)
                    V.reciprocal(lnrs[:, :], lnrs[:, :]).then_inc(dve_step, 1)
                    dve.wait_ge(dve_step, step.up())
                    for m in range(NB):
                        V.scalar_tensor_tensor(out=a_vn[:, m, :], in0=a_vn[:, m, :], scalar=lnrs[:, m:m + 1],
                                               in1=rows[:, R_VG:R_VG + BW], op0=ALU.mult, op1=ALU.mult).then_inc(dve_step, 1)
                        step.up()
                    dve.wait_ge(dve_step, step.now())
                    V.tensor_tensor(a_vn[:, :, :], a_vn[:, :, :],
                                    rows[:, R_VB:R_VB + BW].unsqueeze(1).to_broadcast([P, NB, BW]), ALU.add).then_inc(vn_ready, 1)
                if k == 27:
                    dve.wait_ge(sv_done, 1)
                    for g in range(BT):
                        bs = rows[:, R_BS + g * P:R_BS + g * P + P].unsqueeze(1).to_broadcast([P, NB, P])
                        V.tensor_tensor(a_vn[:, g, :].rearrange("p (m i) -> p m i", m=NB),
                                        psum[:, 2 + g, :].rearrange("p (m i) -> p m i", m=NB), bs, ALU.add).then_inc(dve_step, 1)
                        dve.wait_ge(dve_step, step.up())
                        V.tensor_tensor(a_u[:, g, :], a_u[:, g, :], a_vn[:, g, :], ALU.mult).then_inc(au_ready, 1)
                if k == 29:
                    dve.wait_ge(a_hi, 1)
                    V.tensor_tensor(a_out[:, :, 1, :], a_u[:, :, :], a_out[:, :, 0, :], ALU.subtract).then_inc(a_lo, 1)
                if k == 30:
                    for g, w in enumerate(POOL_WINDOWS):
                        dve.wait_ge(win_ready, g + 1)
                        V.scalar_tensor_tensor(out=c_x[:, g, :], in0=work[:, 2 * (g % 2), :], scalar=1.0 / w,
                                               in1=c_x[:, g, :], op0=ALU.mult, op1=ALU.subtract).then_inc(win_used, 1)
                if k == 32:
                    dve.wait_ge(c_hi, 1)
                    V.tensor_tensor(c_out[:, :, 1, :], c_x[:, :, :], c_out[:, :, 0, :], ALU.subtract).then_inc(c_lo, 1)

            for n in range(N_IN):
                tasks(2 * n)
                lo(n + 1)
                tasks(2 * n + 1)

            def merge(n0, jj, next_width=CW, per_turn=0, turn=None):
                lo(n0 + 5, next_width, per_turn, turn)
                if jj >= 1:
                    dve.wait_ge(m_lo, at(2 * jj, 4, turn))
                for t in range(2):
                    acc, tmp = work[:, 2 * t, :], work[:, 2 * t + 1, :]
                    for b in range(4):
                        i = 4 * t + b
                        if i < 7:
                            dve.wait_ge(y_ready, at(7 * jj + i + 1, 14, turn))
                        else:
                            dve.wait_ge(chunk_done, at(n0 + 5, per_turn, turn))
                        if b == 2:
                            c = V_CS + 2 * jj + t
                            scale = vecs[:, c:c + 1] if turn is None else vecs[:, bass.ds(at(c, 4, turn), 1)]
                        else:
                            scale = UNSCALE
                        V.scalar_tensor_tensor(out=tmp if b else acc, in0=psum[:, 2 + i % 6, :], scalar=scale,
                                               in1=gates[:, b, t, :], op0=ALU.mult, op1=ALU.mult).then_inc(y_used, 1)
                        if b:
                            dve.wait_ge(y_used, at(8 * jj + i + 1, 16, turn))
                            ins = V.tensor_tensor(acc, acc, tmp, ALU.add)
                            if b < 3:
                                ins.then_inc(dve_step, 1)
                                dve.wait_ge(dve_step, step.up())
                            else:
                                ins.then_inc(merged_ready, 1)
                for t in range(2):
                    dve.wait_ge(merged_ready, at(2 * jj + t + 1, 4, turn))
                    dve.wait_ge(m_hi, at(2 * jj + t + 1, 4, turn))
                    j = 2 * jj + t
                    m = merged[:, j] if turn is None else \
                        merged[:, bass.ds(at(j, 4, turn), 1)].rearrange("p o l s -> p (o l) s")
                    V.tensor_tensor(m[:, 1, :], work[:, 2 * t, :], m[:, 0, :], ALU.subtract).then_inc(m_lo, 1)

            def pair_stage(n0, jj, task=None, per_turn=0, turn=None):
                for b in range(4):
                    if task:
                        tasks(2 * (n0 + b))
                    lo(n0 + b + 1, BRW if b == 3 else CW, per_turn, turn)
                    if task:
                        tasks(2 * (n0 + b) + 1)
                merge(n0, jj, CW, per_turn, turn)

            pair_stage(C_G, 0, task=True)
            with dve.Fori(0, 3) as turn:
                step.enter(turn, 8)
                pair_stage(C_G + 5, 1, None, 10, turn)
                pair_stage(C_G + 10, 2, None, 10, turn)
            step.leave(3)
            pair_stage(C_G + 35, 7)

            for n in range(2):
                lo(C_O + n + 1)
            with dve.Fori(0, PAIRS // 2 - 1) as turn:
                lo(C_O + 3, CW, 2, turn)
                lo(C_O + 4, CW, 2, turn)

            inverse_root(2)
            for b in range(PAIRS):
                if b % 4 == 0:
                    dve.wait_ge(res_landed[b // 4], 16)
                V.tensor_tensor(mix[:, 2 * b:2 * b + 2, :], mix[:, 2 * b:2 * b + 2, :],
                                rinv[:, :].unsqueeze(1).to_broadcast([P, 2, S]), ALU.mult).then_inc(dve_step, 1)
                dve.wait_ge(dve_step, step.up())
                for k in (2 * b, 2 * b + 1):
                    V.scalar_tensor_tensor(out=res[:, k, :], in0=mix[:, k, :], scalar=vecs[:, V_POST + k:V_POST + k + 1],
                                           in1=res[:, k, :], op0=ALU.mult, op1=ALU.add).then_inc(x2_ready, 1)
            inverse_root(3)
            normed(res, h2, V_FPRE, 1)

            def ffn_chunk(n0, j0, width, turn):
                lo(n0 + 1, width, 2, turn)
                w = 2 * ((n0 - C_F) % 2)
                dve.wait_ge(evicted1, at(E_F + n0 - C_F + 1, 2, turn))
                V.tensor_tensor(work[:, w, :], work[:, w, :], work[:, w + 1, :], ALU.mult).then_inc(f_ready, 1)
                if n0 == C_F:
                    dve.wait_ge(x2_spilled, 64)
                dve.wait_ge(f_ready, at(j0 + 1, 2, turn))
                dve.wait_ge(f_hi, at(j0 + 1, 2, turn))
                j = at(j0, 2, turn)
                fj = f[:, j] if turn is None else f[:, bass.ds(j, 1)].rearrange("p o l s -> p (o l) s")
                V.tensor_tensor(fj[:, 1, :], work[:, w, :], fj[:, 0, :], ALU.subtract).then_inc(f_lo, 1)

            ffn_chunk(C_F, 0, CW, None)
            ffn_chunk(C_F + 1, 1, CW, None)
            with dve.Fori(0, FT // 2 - 2) as turn:
                ffn_chunk(C_F + 2, 2, CW, turn)
                ffn_chunk(C_F + 3, 3, CW, turn)
            ffn_chunk(C_X - 2, FT - 2, CW, None)
            ffn_chunk(C_X - 1, FT - 1, OW, None)

            with dve.Fori(0, PAIRS - 1) as turn:
                for c in range(OC):
                    lo(C_X + c + 1, OW, OC, turn)
            for c in range(OC - 1):
                lo(C_END - OC + c + 1, OW)

            inverse_root(4)
            for b in range(PAIRS):
                if b % 4 == 0:
                    dve.wait_ge(x2_landed[b // 4], 16)
                V.tensor_tensor(ffn[:, 2 * b:2 * b + 2, :], ffn[:, 2 * b:2 * b + 2, :],
                                rinv[:, :].unsqueeze(1).to_broadcast([P, 2, S]), ALU.mult).then_inc(dve_step, 1)
                dve.wait_ge(dve_step, step.up())
                for k in (2 * b, 2 * b + 1):
                    V.scalar_tensor_tensor(out=x2_back[:, k, :], in0=ffn[:, k, :], scalar=vecs[:, V_FPOST + k:V_FPOST + k + 1],
                                           in1=x2_back[:, k, :], op0=ALU.mult, op1=ALU.add).then_inc(y_out, 1)

        @block.tensor
        def _(pe):
            mm = nc.tensor.matmul

            def three(bank, w_at, slot, hk, start, stop):
                high = whi[:, slot, w_at:w_at + P]
                mm(psum[:, bank, :], high, hk[0], start=start, stop=False)
                mm(psum[:, bank, :], high, hk[1], start=False, stop=False)
                return mm(psum[:, bank, :], wlo[:, slot, w_at:w_at + P], hk[0], start=False, stop=stop)

            def gemm(n0, e0, src, per_turn=0, turn=None, e_per_turn=0, kts=KT, k_from=0,
                     start=True, stop=True, middle=None, ready=None):
                slot = n0 % 2
                pe.wait_ge(lo_ready, at(n0 + 1, per_turn, turn))
                for t in range(2):
                    if start and e0 >= 1:
                        pe.wait_ge(evicted1 if t else evicted0, at(e0, e_per_turn, turn))
                    for k in range(kts):
                        if ready and t == 0:
                            ready(k)
                        hk = (src[:, k_from + k, 0, :], src[:, k_from + k, 1, :])
                        last = three(t, (2 * k + t) * P, slot, hk, start and k == 0, stop and k == kts - 1)
                    if t == 0:
                        if stop:
                            last.then_inc(tile0_done, 1)
                        if middle:
                            middle()
                    else:
                        last.then_inc(chunk_done, 1)

            def gemm_as_it_comes(n0, e0, src, h_base):
                pe.wait_ge(lo_ready, n0 + 1)
                for t in range(2):
                    if e0 >= 1:
                        pe.wait_ge(evicted1 if t else evicted0, e0)
                for k in range(KT):
                    pe.wait_ge(h_lo, h_base + k + 1)
                    for t in range(2):
                        last = three(t, (2 * k + t) * P, n0 % 2, (src[:, k, 0, :], src[:, k, 1, :]), k == 0, k == KT - 1)
                        if k == KT - 1:
                            last.then_inc(chunk_done if t else tile0_done, 1)

            def sum_squares(base):
                for b in range(PAIRS):
                    pe.wait_ge(sq_ready, base + b + 1)
                    for t in range(2):
                        k = 2 * b + t
                        last = mm(psum[:, 7, :], ones[:, :], work[:, 2 * (b % 2) + t, :], start=(k == 0), stop=(k == KT - 1))
                    last.then_inc(sum_ready if b == PAIRS - 1 else sq_used, 1)

            def scores(u):
                m, g = u // 2, u % 2
                half = HALF1 if g else HALF0
                k0 = 0 if m else P
                if u >= 1:
                    pe.wait_ge(s_used, u)
                for p in range(4):
                    last = mm(psum[:, 2 + p // 2, (p % 2) * 2 * P + k0:(p % 2) * 2 * P + 2 * P],
                              query[half, p, m * P:m * P + P], key[half, (m - 1) * P + k0:m * P + P], start=True, stop=True)
                last.then_inc(s_done, 1)

            def prob_transposes(u):
                m0 = 0 if u >= 2 else 1
                pe.wait_ge(prob_ready, u + 1)
                if u >= 1:
                    pe.wait_ge(pt_ready, u)
                for kb in range(m0, 2):
                    for p in range(4):
                        last = nc.tensor.transpose(psum[:, 4 + kb, p * P:p * P + P], prob[:, u % 2, p, kb * P:kb * P + P], ident[:, :])
                last.then_inc(pt_done, 1)

            def heads(u):
                m, g = u // 2, u % 2
                half = HALF1 if g else HALF0
                pe.wait_ge(pt_ready, u + 1)
                if u == 0:
                    pe.wait_ge(vt_ready, 1)
                    pe.wait_ge(cstd_ready, 1)
                else:
                    pe.wait_ge(b_lo, u)
                m0 = 0 if m else 1
                for kb in range(m0, 2):
                    last = mm(psum[half, 6, :], val_tok[:, m - 1 + kb, g * HD:g * HD + HD], prob_t[:, u % 2, kb, :],
                              start=(kb == m0), stop=(kb == 1))
                last.then_inc(pv_done, 1)

            def tasks(k):
                if k == 15:
                    pe.wait_ge(conv_done, 1)
                    for i in range(BT):
                        last = mm(psum[:, 6, :], ones[:, :], conv[:, i, :], start=(i == 0), stop=(i == BT - 1))
                    last.then_inc(mean_done, 1)
                    pe.wait_ge(evicted1, C_B + 3)
                    for m in range(NB):
                        last = nc.tensor.transpose(psum[:, 7, m * P:m * P + P], val[:, m * P:m * P + P], ident[:, :])
                    last.then_inc(vt_done, 1)
                if k == 17:
                    pe.wait_ge(csq_ready, 1)
                    for i in range(BT):
                        last = mm(psum[:, 6, :], ones[:, :], work[:, i, :], start=(i == 0), stop=(i == BT - 1))
                    last.then_inc(var_done, 1)
                if 0 <= k - 15 < 8:
                    scores(k - 15)
                if 0 <= k - 17 < 8:
                    prob_transposes(k - 17)
                if 0 <= k - 18 < 8:
                    heads(k - 18)
                if 0 <= k - 19 < NB:
                    m = k - 19
                    if m == 0:
                        pe.wait_ge(evicted1, C_AV + 2)
                        pe.wait_ge(vt_ready, 1)
                    else:
                        pe.wait_ge(av_used, m)
                    for i in range(BT):
                        last = nc.tensor.transpose(psum[:, 7, i * P:i * P + P], a_v[:, i, m * P:m * P + P], ident[:, :])
                    last.then_inc(av_done, 1)
                if k == 27:
                    pe.wait_ge(vn_ready, 1)
                    pe.wait_ge(wst_masked, 1)
                    pe.wait_ge(pt_ready, 8)
                    for g in range(BT):
                        for m in range(NB):
                            last = mm(psum[:, 2 + g, m * P:m * P + P], a_vn[:, m, g * P:g * P + P], wst[:, g, :], start=True, stop=True)
                    last.then_inc(sv_done, 1)

            def branch(n0, jj, per_turn=0, turn=None):
                slot = n0 % 2
                pe.wait_ge(lo_ready, at(n0 + 1, per_turn, turn))
                for t in range(2):
                    for b, (src, w0, kts) in enumerate(((a_out, 0, BT), (b_out, BT, BT), (c_out, 3 * BT, 1), (d_out, 2 * BT, BT))):
                        i = 4 * t + b
                        if i >= 6:
                            pe.wait_ge(y_used, at(8 * jj + i - 5, 16, turn))
                        elif jj >= 1:
                            pe.wait_ge(y_used, at(8 * jj, 16, turn))
                        for k in range(kts):
                            if b == 2:
                                g = jj // 2
                                hk = [src[:, g, l, :] if turn is None else
                                      src[:, bass.ds(at(g, 1, turn), 1), l, :].rearrange("p o s -> p (o s)") for l in range(2)]
                            else:
                                hk = (src[:, k, 0, :], src[:, k, 1, :])
                            last = three(2 + i % 6, (2 * (w0 + k) + t) * P, slot, hk, k == 0, k == kts - 1)
                        last.then_inc(y_ready if i < 7 else chunk_done, 1)

            pe.wait_ge(consts_ready, 4)
            sum_squares(0)
            gemm_as_it_comes(0, 0, h, 0)
            pe.wait_ge(ident_ready, 1)
            for n in range(1, N_IN):
                gemm(n, n, h, middle=lambda: tasks(2 * n + 1))
                tasks(2 * n + 2)
            for b in range(4):
                n = C_G + b
                gemm(n, n, h, middle=lambda: tasks(2 * n + 1))
                tasks(2 * n + 2)
            pe.wait_ge(a_lo, 1)
            pe.wait_ge(b_lo, 8)
            pe.wait_ge(c_lo, 1)
            pe.wait_ge(d_lo, 1)
            branch(C_G + 4, 0)

            def pair_stage(n0, e0, jj, per_turn=0, turn=None):
                for b in range(4):
                    gemm(n0 + b, e0 + b, h, per_turn, turn, 8)
                branch(n0 + 4, jj, per_turn, turn)

            with pe.Fori(0, 3) as turn:
                pair_stage(C_G + 5, E_G + 4, 1, 10, turn)
                pair_stage(C_G + 10, E_G + 8, 2, 10, turn)
            pair_stage(C_G + 35, E_G + 28, 7)

            def merged_ready_at(k):
                pe.wait_ge(m_lo, k + 1)

            gemm(C_O, E_O, merged, ready=merged_ready_at)
            gemm(C_O + 1, E_O + 1, merged)
            with pe.Fori(0, PAIRS // 2 - 1) as turn:
                for t in range(2):
                    gemm(C_O + 2 + t, E_O + 2 + t, merged, 2, turn, 2)
            pe.wait_ge(osq_used, PAIRS)
            mm(psum[:, 7, :], ones[:, :], std[:, :], start=True, stop=True).then_inc(osum_ready, 1)
            pe.wait_ge(std_ready, 2)
            sum_squares(PAIRS)

            gemm_as_it_comes(C_F, E_F, h2, KT)
            gemm(C_F + 1, E_F + 1, h2)
            with pe.Fori(0, FT // 2 - 1) as turn:
                for t in range(2):
                    gemm(C_F + 2 + t, E_F + 2 + t, h2, 2, turn, 2)
            with pe.Fori(0, PAIRS) as turn:
                for c in range(OC):
                    pe.wait_ge(f_lo, OK * (c + 1))
                    gemm(C_X + c, E_X, f, OC, turn, 1, kts=OK, k_from=OK * c, start=(c == 0), stop=(c == OC - 1))
            pe.wait_ge(osq_used, 2 * PAIRS)
            mm(psum[:, 7, :], ones[:, :], std[:, :], start=True, stop=True).then_inc(osum_ready, 1)


def _chunks(w, order):
    k = w.shape[0] // P
    w = w[:, order].reshape(k, P, -1, 2 * P)
    return np.ascontiguousarray(w.transpose(2, 1, 0, 3)).reshape(-1, P, k * 2 * P)


def kernel(**inputs):
    from concourse import bacc
    from concourse.bass_utils import run_bass_kernel_spmd

    a = {k: np.asarray(v) for k, v in inputs.items()}
    cols = np.arange
    o_b, o_c, o_d = 2 * BW, 2 * BW + 768, 2 * BW + 768 + BW
    order = [np.r_[o_d + i * P:o_d + i * P + P, o_d + BW + i * P:o_d + BW + i * P + P] for i in range(BT)]
    heads = np.concatenate([np.r_[p * HD:p * HD + HD, (p + 4) * HD:(p + 4) * HD + HD] for p in range(4)])
    order += [o_b + heads, cols(o_b + BW, o_c), cols(BW, 2 * BW), cols(0, BW), cols(o_c, o_d)]
    w_in = _chunks(a["w_in"][0], np.concatenate(order))
    every = cols(D)
    w_gate = np.stack([_chunks(a["w_gate"][0, b], every) for b in range(4)], axis=1)
    w_a, w_b, w_d = (_chunks(a[n][0][r], every) for n, r in
                     (("a_w_out", cols(BW)), ("b_w_out", heads), ("d_w_out", cols(BW))))
    w_c = a["c_w_map"][0].reshape(BT, P, 2, 2 * P).transpose(0, 2, 1, 3).reshape(PAIRS, P, 2 * P)
    w_branch = np.concatenate([w_a, w_b, w_d, w_c], axis=2)
    w_o = _chunks(a["w_o"][0], every)
    gu = np.concatenate([np.r_[j * P:j * P + P, DFF + j * P:DFF + j * P + P] for j in range(FT)])
    w_ffn_in = _chunks(a["w_ffn_in"][0], gu)
    w_ffn_out = a["w_ffn_out"][0].reshape(OC, OK, P, PAIRS, 2 * P).transpose(3, 0, 2, 1, 4).reshape(-1, P, OW)

    def by_tile(v):
        return v.reshape(-1, P).T

    vecs = np.concatenate([by_tile(a[n][0]) for n in (
        "norm_mix_pre", "norm_mix_post", "norm_ffn_pre", "norm_ffn_post", "c_scale", "b_gate",
        "d_w_dw", "d_b_dw", "d_ln_g", "d_ln_b")], axis=1)
    rows = np.concatenate([a[n][0].reshape(-1) for n in ("a_vnorm_g", "a_vnorm_b", "a_b_s", "b_sinks")])
    x = a["x"][0].T.reshape(KT, P, S).transpose(1, 0, 2)
    ws = a["a_w_s"][0].transpose(2, 0, 1)

    arrays = {"x_t": x, "w_in_chunks": w_in, "w_gate_chunks": w_gate, "w_branch_chunks": w_branch,
              "w_o_chunks": w_o, "w_ffn_in_chunks": w_ffn_in, "w_ffn_out_chunks": w_ffn_out,
              "vectors": vecs, "row_vectors": rows, "w_s_t": ws}
    arrays = {n: np.ascontiguousarray(v) for n, v in arrays.items()}
    nc = bacc.Bacc("TRN2", target_bir_lowering=False, num_devices=1)
    args = [nc.dram_tensor(n, v.shape, mybir.dt.from_np(v.dtype), kind="ExternalInput").ap() for n, v in arrays.items()]
    out = nc.dram_tensor("out_t", (P, KT, S), F32, kind="ExternalOutput").ap()
    x2_spill = nc.dram_tensor("x2_spill", (P, KT, S), F32).ap()
    block_program(nc, *args, out, x2_spill)
    r = run_bass_kernel_spmd(nc, [arrays], core_ids=[0])
    got = np.asarray(r.results[0]["out_t"])
    return np.ascontiguousarray(got.transpose(1, 0, 2).reshape(D, S).T)[None]
```

```python
from contextlib import ExitStack

import numpy as np

import concourse.bass as bass
from concourse import mybir

F32 = mybir.dt.float32
F16 = mybir.dt.float16
I32 = mybir.dt.int32
ALU = mybir.AluOpType
ACT = mybir.ActivationFunctionType
AX = mybir.AxisListType

P = 128
D = 2048
S = 512
KT = D // P
BW = 512
BT = BW // P
NB = S // P
DFF = 5632
FT = DFF // P
HD = 64
CONV_W = 31
POOL_WINDOWS = (2, 4, 8, 16)
CHUNK = 64
RMS_EPS, LN_EPS = 1e-6, 1e-5
MASKED = -1e30
DVE_PAIRS = (0, 1, 2)
PE_PAIRS = (3, 4, 5)
POOL_PAIRS = (6, 7)
PE_BANKS = (0, 1, 2, 3, 4, 7)
FFN_TURNS = 10
WSCALE = 256.0
UNSCALE = 1.0 / WSCALE

CW = KT * 2 * P
BRW = (3 * BT + 1) * 2 * P
OK = 11
OC = FT // OK
OW = OK * 2 * P
N_IN = 13
PAIRS = KT // 2
C_D, C_B, C_AV, C_AU, C_C = 0, 4, 7, 9, 11
C_G = N_IN
C_O = C_G + 5 * PAIRS
C_F = C_O + PAIRS
C_X = C_F + FT
C_END = C_X + OC * PAIRS

E_G = N_IN
E_O = E_G + 4 * PAIRS
E_F = E_O + PAIRS
E_X = E_F + FT

V_PRE, V_POST, V_FPRE, V_FPOST, V_CS = 0, KT, 2 * KT, 3 * KT, 4 * KT
V_BG = 5 * KT
V_DW = V_BG + 4 * KT
V_DB = V_DW + CONV_W * BT
V_LG = V_DB + BT
V_LB = V_LG + BT
NV = V_LB + BT
R_VG, R_VB, R_BS, R_SK = 0, BW, 2 * BW, 3 * BW
NR = 3 * BW + 8

HALF0, HALF1 = slice(0, 64), slice(64, 128)


class Count:

    def __init__(self):
        self.n, self.turn, self.per_turn = 0, None, 0

    def up(self):
        self.n += 1
        return self.now()

    def now(self):
        return self.n if self.turn is None else self.turn * self.per_turn + self.n

    def enter(self, turn, per_turn):
        self.turn, self.per_turn, self.start = turn, per_turn, self.n

    def leave(self, turns):
        assert self.n - self.start == self.per_turn, (self.n, self.start)
        self.n, self.turn = self.start + self.per_turn * turns, None


def at(base, per_turn=0, turn=None):
    return base if turn is None else turn * per_turn + base


def block_program(nc, x, w_in, w_gate, w_branch, w_o, w_ffn_in, w_ffn_out, vecs_d, rows_d, ws_d,
                  out, x2_spill):
    with ExitStack() as ctx:
        def sb(name, shape, dt):
            return ctx.enter_context(nc.sbuf_tensor(name, shape, dt))

        def sem(name):
            return ctx.enter_context(nc.semaphore(name))

        stage = sb("stage", [P, 2, CW], F32)
        whi = sb("whi", [P, 2, CW], F16)
        wlo = sb("wlo", [P, 2, CW], F16)
        region_a = sb("region_a", [P, FT * S], F32)
        region_b = sb("region_b", [P, KT * S], F32)
        work = sb("work", [P, 4, S], F32)
        vecs = sb("vecs", [P, NV], F32)
        rows = sb("rows", [P, NR], F32)
        wst = sb("wst", [P, BT, P], F32)
        ident = sb("ident", [P, P], F32)
        ones = sb("ones", [P, P], F32)
        mask = sb("mask", [P, 2 * P], F32)
        rms = sb("rms", [P, 4, NB], F32)
        irms = sb("irms", [P, 4, NB], F32)
        rinv_sb = sb("rinv_sb", [P, S], F32)
        std = sb("std", [P, S], F32)
        lnstat = sb("lnstat", [P, NB, 6], F32)
        lnmv = sb("lnmv", [P, NB, 2], F32)
        lnrs = sb("lnrs", [P, NB], F32)
        smax = sb("smax", [P, 4, 4], F32)
        poolfix = sb("poolfix", [P, 4, 16], F32)
        posi = sb("posi", [P, 16], I32)
        warm = sb("warm", [P, 1], F32)

        def view(region, start, n, dt, pattern=None, **sizes):
            v = region[:, start:start + n]
            if dt != F32:
                v = v.bitcast(dt)
            return v.rearrange(pattern, **sizes) if pattern else v

        K2 = KT * S
        h = view(region_a, 0, K2, F16, "p (k l s) -> p k l s", k=KT, l=2)
        b2 = BT * S
        a_out, b_out, c_out, d_out = (
            view(region_a, K2 + i * b2, b2, F16, "p (k l s) -> p k l s", k=BT, l=2) for i in range(4))
        a_v = view(region_a, K2, b2, F32, "p (k s) -> p k s", k=BT)
        key = view(region_a, K2 + 2 * b2, S, F32)
        val = view(region_a, K2 + 2 * b2 + S, S, F32)
        val_tok = view(region_a, K2 + 2 * b2 + 2 * S, S, F32, "p (m d) -> p m d", m=NB)
        glu = view(region_a, K2 + 3 * b2, b2, F32, "p (k s) -> p k s", k=BT)
        gate_at = K2 + 4 * b2
        gates = view(region_a, gate_at, 8 * S, F32, "p (b t s) -> p b t s", b=4, t=2)
        query = view(region_a, gate_at, b2, F32, "p (k s) -> p k s", k=BT)
        prob = view(region_a, gate_at + b2, b2, F32, "p (u k j) -> p u k j", u=2, k=4)
        c_x = view(region_a, gate_at + 8 * S, b2, F32, "p (k s) -> p k s", k=BT)
        mix = view(region_a, 0, K2, F32, "p (k s) -> p k s", k=KT)
        res = view(region_a, K2, K2, F32, "p (k s) -> p k s", k=KT)
        f = view(region_a, 0, FT * S, F16, "p (k l s) -> p k l s", k=FT, l=2)
        x_in = view(region_b, 0, K2, F32, "p (k s) -> p k s", k=KT)
        conv = view(region_b, 0, b2, F32, "p (k s) -> p k s", k=BT)
        prob_t = view(region_b, b2, b2, F32, "p (u m q) -> p u m q", u=2, m=2)
        a_vn = view(region_b, 2 * b2, b2, F32, "p (m c) -> p m c", m=NB)
        a_u = view(region_b, 3 * b2, b2, F32, "p (k s) -> p k s", k=BT)
        merged = view(region_b, 0, K2, F16, "p (k l s) -> p k l s", k=KT, l=2)
        h2 = merged
        ffn = x_in
        x2_back = stage[:, :, :].rearrange("p u (k s) -> p (u k) s", s=S)

        psum = ctx.enter_context(nc.psum_tensor("psum", [P, 8, S], F32))
        rinv = psum[:, 6, :]

        x_landed = [sem(f"x_landed{i}") for i in range(4)]
        vecs_landed, rows_landed, ws_landed = sem("vecs_landed"), sem("rows_landed"), sem("ws_landed")
        w_landed = [sem(f"w_landed{i}") for i in range(2)]
        res_landed = [sem(f"res_landed{i}") for i in range(2)]
        x2_spilled, x2_landed = sem("x2_spilled"), [sem(f"x2_landed{i}") for i in range(2)]
        out_stored = sem("out_stored")
        consts_ready, ident_zero, ident_ready, posi_ready = (
            sem("consts_ready"), sem("ident_zero"), sem("ident_ready"), sem("posi_ready"))
        cs_ready, wst_masked = sem("cs_ready"), sem("wst_masked")
        hi_ready, lo_ready = sem("hi_ready"), sem("lo_ready")
        tile0_done = sem("tile0_done")
        chunk_done = sem("chunk_done")
        evicted0, evicted1 = sem("evicted0"), sem("evicted1")
        sq_ready, sq_used = sem("sq_ready"), sem("sq_used")
        sum_ready, rms_ready, rinv_ready = sem("sum_ready"), sem("rms_ready"), sem("rinv_ready")
        irms_ready, rinv_copied = sem("irms_ready"), sem("rinv_copied")
        xr_ready, h_hi, h_lo = sem("xr_ready"), sem("h_hi"), sem("h_lo")
        piece_hi, piece_lo = sem("piece_hi"), sem("piece_lo")
        mix_scaled = sem("mix_scaled")
        glu_ready = sem("glu_ready")
        conv_done, mean_done, centered, csq_ready, var_done, cstd_ready, cnorm_ready, silu_ready, d_hi, d_lo = (
            sem(n) for n in ("conv_done", "mean_done", "centered", "csq_ready", "var_done",
                             "cstd_ready", "cnorm_ready", "silu_ready", "d_hi", "d_lo"))
        vt_done, vt_ready, s_done, s_used, s_shift, exp_ready, prob_ready, pt_done, pt_ready = (
            sem(n) for n in ("vt_done", "vt_ready", "s_done", "s_used", "s_shift", "exp_ready",
                             "prob_ready", "pt_done", "pt_ready"))
        pv_done, b_hi, b_lo = sem("pv_done"), sem("b_hi"), sem("b_lo")
        av_done, av_used, lnvar_ready, lnstd_ready, vn_ready, sv_done, au_ready, a_hi, a_lo = (
            sem(n) for n in ("av_done", "av_used", "lnvar_ready", "lnstd_ready", "vn_ready",
                             "sv_done", "au_ready", "a_hi", "a_lo"))
        win_ready, win_used, c_hi, c_lo = (
            sem(n) for n in ("win_ready", "win_used", "c_hi", "c_lo"))
        y_ready, y_used, merged_ready, m_hi, m_lo = (
            sem(n) for n in ("y_ready", "y_used", "merged_ready", "m_hi", "m_lo"))
        osq_ready, osq_used, osum_ready = sem("osq_ready"), sem("osq_used"), sem("osum_ready")
        x2_ready, x2sq_used, f_silu, f_ready, f_hi, f_lo, y_out, y_scaled, y_pool, y_sum, y_act = (
            sem(n) for n in ("x2_ready", "x2sq_used", "f_silu", "f_ready", "f_hi", "f_lo", "y_out", "y_scaled", "y_pool", "y_sum", "y_act"))
        act_step, dve_step, pool_step = sem("act_step"), sem("dve_step"), sem("pool_step")

        block = ctx.enter_context(nc.Block())

        @block.sync
        def _(sp):
            def load(n0, src, width=CW, per_turn=0, turn=None):
                if n0 >= 2:
                    sp.wait_ge(lo_ready, at(n0 - 1, per_turn, turn))
                sp.dma_start(stage[:, n0 % 2, 0:width], src).then_inc(w_landed[n0 % 2], 16)

            def pair_stage(n0, jj, per_turn=0, turn=None):
                j = at(jj, 2, turn)
                for b in range(4):
                    src = w_gate[jj, b] if turn is None else \
                        w_gate[bass.ds(j, 1), b].rearrange("o p n -> (o p) n")
                    load(n0 + b, src, CW, per_turn, turn)
                src = w_branch[jj] if turn is None else \
                    w_branch[bass.ds(j, 1)].rearrange("o p n -> (o p) n")
                load(n0 + 4, src, BRW, per_turn, turn)

            def one(w, i):
                return w[bass.ds(i, 1)].rearrange("o p n -> (o p) n")

            sp.dma_start(vecs[:, :], vecs_d).then_inc(vecs_landed, 16)
            for i in range(4):
                sp.dma_start(x_in[:, 4 * i:4 * i + 4, :], x[:, 4 * i:4 * i + 4, :]).then_inc(x_landed[i], 16)
            load(0, w_in[0])
            load(1, w_in[1])
            sp.dma_start(rows[:, :], rows_d.partition_broadcast(P)).then_inc(rows_landed, 16)
            sp.dma_start(wst[:, :, :], ws_d).then_inc(ws_landed, 16)
            for n in range(2, N_IN):
                load(n, w_in[n])
            pair_stage(C_G, 0)
            with sp.Fori(0, 3) as turn:
                pair_stage(C_G + 5, 1, 10, turn)
                pair_stage(C_G + 10, 2, 10, turn)
            pair_stage(C_G + 35, 7)
            load(C_O, w_o[0])
            load(C_O + 1, w_o[1])
            sp.wait_ge(chunk_done, C_O)
            for i in range(2):
                sp.dma_start(res[:, 8 * i:8 * i + 8, :], x[:, 8 * i:8 * i + 8, :]).then_inc(res_landed[i], 16)
            with sp.Fori(0, PAIRS // 2 - 1) as turn:
                for t in range(2):
                    load(C_O + 2 + t, one(w_o, at(2 + t, 2, turn)), CW, 2, turn)
            load(C_F, w_ffn_in[0])
            load(C_F + 1, w_ffn_in[1])
            for i in range(4):
                sp.wait_ge(x2_ready, 4 * i + 4)
                sp.dma_start(x2_spill[:, 4 * i:4 * i + 4, :], res[:, 4 * i:4 * i + 4, :]).then_inc(x2_spilled, 16)
            with sp.Fori(0, FT // 2 - 1) as turn:
                for t in range(2):
                    load(C_F + 2 + t, one(w_ffn_in, at(2 + t, 2, turn)), CW, 2, turn)
            with sp.Fori(0, PAIRS) as turn:
                for c in range(OC):
                    load(C_X + c, one(w_ffn_out, at(c, OC, turn)), OW, OC, turn)
            sp.wait_ge(x2_spilled, 64)
            for i in (1, 0):
                sp.wait_ge(lo_ready, C_END - i)
                sp.dma_start(x2_back[:, 8 * i:8 * i + 8, :], x2_spill[:, 8 * i:8 * i + 8, :]).then_inc(x2_landed[i], 16)

            def store(b):
                sp.dma_start(out[:, 2 * b:2 * b + 2, :], x2_back[:, 2 * b:2 * b + 2, :]).then_inc(out_stored, 16)

            for by, i in ((y_out, 0), (y_act, 0), (y_out, 1), (y_pool, 0), (y_act, 1), (y_out, 2), (y_pool, 1), (y_act, 2)):
                sp.wait_ge(by, (2 if by is y_act else 1) * (i + 1))
                store((PE_PAIRS if by is y_act else POOL_PAIRS if by is y_pool else DVE_PAIRS)[i])
            sp.wait_ge(out_stored, 16 * PAIRS)

        @block.gpsimd
        def _(pool):
            step = Count()
            nc.gpsimd.memset(ones[:, :], 1.0).then_inc(consts_ready, 1)
            nc.gpsimd.memset(ident[:, :], 0.0).then_inc(ident_zero, 1)
            nc.gpsimd.memset(mask[:, :], 0.0).then_inc(pool_step, 1)
            pool.wait_ge(pool_step, step.up())
            nc.gpsimd.memset(mask[HALF0, 0:CHUNK], MASKED).then_inc(consts_ready, 1)
            nc.gpsimd.memset(mask[HALF0, 3 * CHUNK:4 * CHUNK], MASKED).then_inc(consts_ready, 1)
            pool.wait_ge(consts_ready, 3)
            nc.gpsimd.memset(mask[HALF1, 0:2 * CHUNK], MASKED).then_inc(consts_ready, 1)
            pool.wait_ge(consts_ready, 4)
            pool.wait_ge(ident_zero, 1)
            nc.gpsimd.affine_select(out=ident[:, :], in_=ident[:, :], compare_op=ALU.not_equal, fill=1.0,
                                    base=0, pattern=[[-1, P]], channel_multiplier=1).then_inc(ident_ready, 1)
            nc.gpsimd.iota(posi[:, :], [[1, 16]], base=1, channel_multiplier=0).then_inc(posi_ready, 1)
            pool.wait_ge(ws_landed, 16)
            pool.wait_ge(ident_ready, 1)
            pool.wait_ge(posi_ready, 1)
            nc.gpsimd.memset(wst[HALF1, :, 0:CHUNK], 0.0).then_inc(wst_masked, 1)
            pool.wait_ge(wst_masked, 1)

            for i in range(BT):
                pool.wait_ge(evicted1, i + 1)
                nc.gpsimd.tensor_tensor(glu[:, i, :], work[:, 2 * (i % 2), :], work[:, 2 * (i % 2) + 1, :],
                                        ALU.mult).then_inc(glu_ready, 1)

            pool.wait_ge(evicted1, C_C + 2)
            for g in range(BT):
                if g >= 2:
                    pool.wait_ge(win_used, g - 1)
                src = c_x[:, g, :]
                for k in range(g + 1):
                    d = 1 << k
                    dst = work[:, 2 * (g % 2) + (g - k) % 2, :]
                    nc.gpsimd.tensor_copy(dst[:, 0:d], src[:, 0:d]).then_inc(pool_step, 1)
                    step.up()
                    last = nc.gpsimd.tensor_tensor(dst[:, d:S], src[:, d:S], src[:, 0:S - d], ALU.add)
                    last.then_inc(pool_step, 1)
                    pool.wait_ge(pool_step, step.up())
                    src = dst
                pool.wait_ge(posi_ready, 2)
                nc.gpsimd.tensor_tensor(src[:, 0:16], src[:, 0:16], poolfix[:, g, :], ALU.mult).then_inc(win_ready, 1)

            for phase in range(2):
                if phase == 1:
                    pool.wait_ge(osum_ready, 1)
                    nc.gpsimd.memset(std[:, :], 0.0).then_inc(pool_step, 1)
                    pool.wait_ge(pool_step, step.up())
                    for b in range(PAIRS):
                        pool.wait_ge(sq_ready, PAIRS + b + 1)
                        nc.gpsimd.tensor_tensor(std[:, :], std[:, :], work[:, 2 * (b % 2), :], ALU.add).then_inc(pool_step, 1)
                        pool.wait_ge(pool_step, step.up())
                        nc.gpsimd.tensor_tensor(std[:, :], std[:, :], work[:, 2 * (b % 2) + 1, :], ALU.add).then_inc(x2sq_used, 1)
                        pool.wait_ge(x2sq_used, b + 1)
                if phase == 0:
                    pool.wait_ge(m_lo, KT)
                else:
                    pool.wait_ge(sum_ready, 2)
                nc.gpsimd.memset(std[:, :], 0.0).then_inc(pool_step, 1)
                pool.wait_ge(pool_step, step.up())
                with pool.Fori(0, PAIRS) as turn:
                    step.enter(turn, 1)
                    for t in range(2):
                        pool.wait_ge(osq_ready, at(2 * PAIRS * phase + t + 1, 2, turn))
                        if t == 1:
                            pool.wait_ge(pool_step, step.up())
                        ins = nc.gpsimd.tensor_tensor(std[:, :], std[:, :], work[:, t, :], ALU.add)
                        ins.then_inc(pool_step if t == 0 else osq_used, 1)
                    pool.wait_ge(osq_used, at(PAIRS * phase + 1, 1, turn))
                step.leave(PAIRS)

            pool.wait_ge(rinv_copied, 2)
            pool.wait_ge(x2_landed[1], 16)
            pool.wait_ge(evicted1, E_X + PAIRS)
            for b in POOL_PAIRS:
                two = slice(2 * b, 2 * b + 2)
                nc.gpsimd.tensor_tensor(ffn[:, two, :], ffn[:, two, :],
                                        rinv_sb[:, :].unsqueeze(1).to_broadcast([P, 2, S]), ALU.mult).then_inc(pool_step, 1)
                pool.wait_ge(pool_step, step.up())
                nc.gpsimd.tensor_tensor(x2_back[:, two, :], x2_back[:, two, :], ffn[:, two, :], ALU.add).then_inc(y_pool, 1)

        @block.scalar
        def _(act):
            step = Count()

            def hi(n0, width=CW, per_turn=0, turn=None):
                act.wait_ge(w_landed[n0 % 2], at(16 * (n0 // 2 + 1), 8 * per_turn, turn))
                if n0 >= 2:
                    act.wait_ge(chunk_done, at(n0 - 1, per_turn, turn))
                nc.scalar.activation(whi[:, n0 % 2, 0:width], stage[:, n0 % 2, 0:width], ACT.Copy,
                                     scale=WSCALE).then_inc(hi_ready, 1)

            def hi_pieces(n0, pieces=range(4)):
                if 0 in pieces:
                    act.wait_ge(w_landed[n0 % 2], 16 * (n0 // 2 + 1))
                    if n0 >= 2:
                        act.wait_ge(chunk_done, n0 - 1)
                for i in pieces:
                    at_ = slice(i * CW // 4, (i + 1) * CW // 4)
                    nc.scalar.activation(whi[:, n0 % 2, at_], stage[:, n0 % 2, at_], ACT.Copy,
                                         scale=WSCALE).then_inc(piece_hi if i < 3 else hi_ready, 1)

            def evict0(e0, dst, func=ACT.Identity, per_turn=0, turn=None, **kw):
                act.wait_ge(tile0_done, at(e0 + 1, per_turn, turn))
                nc.scalar.activation(dst, psum[:, 0, :], func, scale=UNSCALE, **kw).then_inc(evicted0, 1)

            def evict1(n0, dst, func=ACT.Identity, per_turn=0, turn=None, **kw):
                act.wait_ge(chunk_done, at(n0 + 1, per_turn, turn))
                nc.scalar.activation(dst, psum[:, 1, :], func, scale=UNSCALE, **kw).then_inc(evicted1, 1)

            def mean_root(src, n, eps, done, value, ready):
                act.wait_ge(done, value)
                nc.scalar.activation(std[:, :], src, ACT.Sqrt, scale=1.0 / n, bias=eps).then_inc(ready, 1)

            def norm_root(i, src, done, value):
                act.wait_ge(done, value)
                nc.scalar.activation(rms[:, i, :], src, ACT.Sqrt, scale=1.0 / D, bias=RMS_EPS).then_inc(rms_ready, 1)

            def load_sqrt_table():
                nc.scalar.activation(warm[:, :], ones[:, 0:1], ACT.Sqrt).then_inc(act_step, 1)

            act.wait_ge(consts_ready, 1)
            load_sqrt_table()
            for b in range(PAIRS):
                if b % 2 == 0:
                    act.wait_ge(x_landed[b // 2], 16)
                if b >= 2:
                    act.wait_ge(sq_used, b - 1)
                nc.scalar.activation(work[:, 2 * (b % 2):2 * (b % 2) + 2, :], x_in[:, 2 * b:2 * b + 2, :],
                                     ACT.Square).then_inc(sq_ready, 1)
            norm_root(0, psum[:, 7, 0:NB], sum_ready, 1)

            for k in range(KT):
                if k % 4 == 0:
                    hi_pieces(0, (k // 4,))
                act.wait_ge(xr_ready, k + 1 if k < 2 else 2 * (k // 2) + 2)
                nc.scalar.activation(h[:, k, 0, :], work[:, k % 4, :], ACT.Copy,
                                     scale=vecs[:, V_PRE + k:V_PRE + k + 1]).then_inc(h_hi, 1)

            def exp_part(u):
                act.wait_ge(s_shift, u + 1)
                lo_key = 0 if u >= 2 else P
                nc.scalar.activation(prob[:, u % 2, :, lo_key:], prob[:, u % 2, :, lo_key:], ACT.Exp).then_inc(exp_ready, 1)
                nc.scalar.activation(smax[:, 1, :], smax[:, 1, :], ACT.Exp).then_inc(exp_ready, 1)

            def evict_prob_t(u):
                act.wait_ge(pt_done, u + 1)
                if u >= 2:
                    act.wait_ge(pv_done, u - 1)
                m0 = 0 if u >= 2 else 1
                nc.scalar.activation(prob_t[:, u % 2, m0:, :], psum[:, 4 + m0:6, :], ACT.Copy).then_inc(pt_ready, 1)

            def heads_high(u):
                m, g = u // 2, u % 2
                half = HALF1 if g else HALF0
                act.wait_ge(pv_done, u + 1)
                nc.scalar.activation(b_out[half, :, 0, m * P:m * P + P],
                                     psum[half, 6, :].rearrange("p (k q) -> p k q", k=4), ACT.Copy).then_inc(b_hi, 1)

            def tasks(k):
                if k == 16:
                    act.wait_ge(centered, 1)
                    nc.scalar.activation(work[:, :, :], conv[:, :, :], ACT.Square).then_inc(csq_ready, 1)
                if k == 15:
                    act.wait_ge(vt_done, 1)
                    nc.scalar.activation(val_tok[:, :, :], psum[:, 7, :].rearrange("p (m d) -> p m d", m=NB),
                                         ACT.Copy).then_inc(vt_ready, 1)
                if k == 17:
                    mean_root(psum[:, 6, :], BW, LN_EPS, var_done, 1, cstd_ready)
                if k == 18:
                    act.wait_ge(cnorm_ready, 1)
                    for i in range(BT):
                        nc.scalar.activation(conv[:, i, :], conv[:, i, :], ACT.Silu,
                                             scale=vecs[:, V_LG + i:V_LG + i + 1],
                                             bias=vecs[:, V_LB + i:V_LB + i + 1]).then_inc(silu_ready, 1)
                    act.wait_ge(silu_ready, BT)
                    nc.scalar.activation(d_out[:, :, 0, :], conv[:, :, :], ACT.Copy).then_inc(d_hi, 1)
                if 0 <= k - 17 < 8:
                    evict_prob_t(k - 17)
                if 0 <= k - 18 < 8:
                    heads_high(k - 18)
                if 0 <= k - 15 < 8:
                    exp_part(k - 15)
                if k == 25:
                    act.wait_ge(lnvar_ready, NB)
                    nc.scalar.activation(lnrs[:, :], lnmv[:, :, 1], ACT.Sqrt, bias=LN_EPS).then_inc(lnstd_ready, 1)
                if k == 29:
                    act.wait_ge(au_ready, BT)
                    nc.scalar.activation(a_out[:, :, 0, :], a_u[:, :, :], ACT.Copy).then_inc(a_hi, 1)
                if k == 32:
                    act.wait_ge(win_used, BT)
                    nc.scalar.activation(c_out[:, :, 0, :], c_x[:, :, :], ACT.Copy).then_inc(c_hi, 1)

            def evictions(n):
                if n < C_B:
                    if n >= 2:
                        act.wait_ge(glu_ready, n - 1)
                    return [(work[:, 2 * (n % 2), :], ACT.Identity), (work[:, 2 * (n % 2) + 1, :], ACT.Sigmoid)]
                if n < C_B + 2:
                    return [(query[:, 2 * (n - C_B) + t, :], ACT.Identity) for t in range(2)]
                if n == C_B + 2:
                    return [(key, ACT.Identity), (val, ACT.Identity)]
                if n < C_C:
                    dst, i = (a_v, n - C_AV) if n < C_AU else (a_u, n - C_AU)
                    return [(dst[:, 2 * i + t, :], ACT.Gelu) for t in range(2)]
                return [(c_x[:, 2 * (n - C_C) + t, :], ACT.Identity) for t in range(2)]

            for n in range(N_IN):
                if n == 0:
                    hi_pieces(1)
                else:
                    hi(n + 1)
                tasks(2 * n)
                to = evictions(n)
                evict0(n, *to[0])
                tasks(2 * n + 1)
                evict1(n, *to[1])

            def pair_stage(n0, e0, jj, task=None, per_turn=0, turn=None, next_width=CW):
                ept = 8 if turn is not None else 0
                for b in range(4):
                    hi(n0 + b + 1, BRW if b == 3 else CW, per_turn, turn)
                    if task:
                        tasks(2 * (n0 + b))
                    if b == 0 and jj >= 1:
                        act.wait_ge(y_used, at(8 * jj, 16, turn))
                    for t, ev in ((0, evict0), (1, evict1)):
                        col = V_BG + b * KT + 2 * jj + t
                        bias = vecs[:, col:col + 1] if turn is None else vecs[:, bass.ds(at(col, 4, turn), 1)]
                        if t == 0:
                            evict0(e0 + b, gates[:, b, 0, :], ACT.Sigmoid, ept, turn, bias=bias)
                            if task:
                                tasks(2 * (n0 + b) + 1)
                        else:
                            evict1(n0 + b, gates[:, b, 1, :], ACT.Sigmoid, per_turn, turn, bias=bias)
                hi(n0 + 5, next_width, per_turn, turn)
                for t in range(2):
                    act.wait_ge(merged_ready, at(2 * jj + t + 1, 4, turn))
                    j = 2 * jj + t
                    dst = merged[:, j, 0, :] if turn is None else \
                        merged[:, bass.ds(at(j, 4, turn), 1), 0, :].rearrange("p o s -> p (o s)")
                    nc.scalar.activation(dst, work[:, 2 * t, :], ACT.Copy).then_inc(m_hi, 1)

            pair_stage(C_G, E_G, 0, task=True)
            with act.Fori(0, 3) as turn:
                pair_stage(C_G + 5, E_G + 4, 1, None, 10, turn)
                pair_stage(C_G + 10, E_G + 8, 2, None, 10, turn)
            pair_stage(C_G + 35, E_G + 28, 7)

            def norm_pair(n0, e0, dst, gain, j0, phase, pairs_before, pairs_per_turn, per_turn, turn):
                for t in range(2):
                    if t == 0:
                        act.wait_ge(tile0_done, at(e0 + 1, pairs_per_turn, turn))
                        if pairs_before > 0:
                            act.wait_ge(osq_used, at(PAIRS * phase + pairs_before, pairs_per_turn, turn))
                    else:
                        act.wait_ge(chunk_done, at(n0 + 1, per_turn, turn))
                    nc.scalar.activation(work[:, t, :], psum[:, t, :], ACT.Square, scale=UNSCALE).then_inc(osq_ready, 1)
                    j = at(j0 + t, 2 * pairs_per_turn, turn)
                    d = dst[:, j, :] if turn is None else dst[:, bass.ds(j, 1), :].rearrange("p o s -> p (o s)")
                    g = vecs[:, gain + j:gain + j + 1] if turn is None else vecs[:, bass.ds(j + gain, 1)]
                    nc.scalar.activation(d, psum[:, t, :], ACT.Copy, scale=g).then_inc(evicted1 if t else evicted0, 1)

            def o_chunk(n0, e0, j0, pairs_before, turn):
                hi(n0 + 1, CW, 2, turn)
                norm_pair(n0, e0, mix, V_POST, j0, 0, pairs_before, 2, 2, turn)

            act.wait_ge(act_step, 1)
            load_sqrt_table()
            o_chunk(C_O, E_O, 0, 0, None)
            o_chunk(C_O + 1, E_O + 1, 2, 1, None)
            with act.Fori(0, PAIRS // 2 - 1) as turn:
                o_chunk(C_O + 2, E_O + 2, 4, 2, turn)
                o_chunk(C_O + 3, E_O + 3, 6, 3, turn)

            hi_pieces(C_F + 1, (0, 1))
            norm_root(1, psum[:, 7, 0:NB], osum_ready, 1)
            for b in range(PAIRS):
                for k in (2 * b, 2 * b + 1):
                    act.wait_ge(x2_ready, k + 1 if b == 0 else 2 * b + 2)
                    nc.scalar.activation(h2[:, k, 0, :], res[:, k, :], ACT.Copy,
                                         scale=vecs[:, V_FPRE + k:V_FPRE + k + 1]).then_inc(h_hi, 1)
                if b >= 2:
                    act.wait_ge(x2sq_used, b - 1)
                nc.scalar.activation(work[:, 2 * (b % 2):2 * (b % 2) + 2, :], res[:, 2 * b:2 * b + 2, :],
                                     ACT.Square).then_inc(sq_ready, 1)
                if b in (1, 3):
                    hi_pieces(C_F + 1, (2 + b // 2,))
            norm_root(2, psum[:, 7, 0:NB], sum_ready, 2)
            hi_pieces(C_F + 2)

            def ffn_chunk(n0, j0, width, turn):
                if n0 > C_F + 1:
                    hi(n0 + 1, width, 2, turn)
                w = 2 * ((n0 - C_F) % 2)
                act.wait_ge(evicted0, at(E_F + j0 + 1, 2, turn))
                nc.scalar.activation(work[:, w, :], work[:, w, :], ACT.Silu, scale=UNSCALE).then_inc(f_silu, 1)
                act.wait_ge(f_ready, at(j0 + 1, 2, turn))
                j = at(j0, 2, turn)
                dst = f[:, j, 0, :] if turn is None else \
                    f[:, bass.ds(j, 1), 0, :].rearrange("p o s -> p (o s)")
                nc.scalar.activation(dst, work[:, w, :], ACT.Copy).then_inc(f_hi, 1)

            ffn_chunk(C_F, 0, CW, None)
            ffn_chunk(C_F + 1, 1, CW, None)
            with act.Fori(0, FT // 2 - 2) as turn:
                ffn_chunk(C_F + 2, 2, CW, turn)
                ffn_chunk(C_F + 3, 3, CW, turn)
            ffn_chunk(C_X - 2, FT - 2, CW, None)
            ffn_chunk(C_X - 1, FT - 1, OW, None)

            def out_pair(n0, e0, j0, pairs_before, last, turn):
                for c in range(OC):
                    if not (last and c == OC - 1):
                        hi(n0 + c + 1, OW, OC, turn)
                if pairs_before == 0:
                    act.wait_ge(f_lo, FT)
                norm_pair(n0 + OC - 1, e0, ffn, V_FPOST, j0, 1, pairs_before, 1, OC, turn)

            act.wait_ge(act_step, 2)
            load_sqrt_table()
            out_pair(C_X, E_X, 0, 0, False, None)
            with act.Fori(0, PAIRS - 2) as turn:
                out_pair(C_X + OC, E_X + 1, 2, 1, False, turn)
            out_pair(C_END - OC, E_X + PAIRS - 1, KT - 2, PAIRS - 1, True, None)
            norm_root(3, psum[:, 7, 0:NB], osum_ready, 2)
            act.wait_ge(rinv_ready, 5)
            nc.scalar.activation(rinv_sb[:, :], psum[:, 5, :], ACT.Copy).then_inc(rinv_copied, 1)
            for i, bank in enumerate(PE_BANKS):
                act.wait_ge(y_sum, i + 1)
                nc.scalar.activation(x2_back[:, 2 * PE_PAIRS[0] + i, :], psum[:, bank, :], ACT.Copy).then_inc(y_act, 1)

        @block.vector
        def _(dve):
            step = Count()
            V = nc.vector

            def lo(n0, width=CW, per_turn=0, turn=None):
                dve.wait_ge(hi_ready, at(n0 + 1, per_turn, turn))
                V.scalar_tensor_tensor(out=wlo[:, n0 % 2, 0:width], in0=stage[:, n0 % 2, 0:width], scalar=WSCALE,
                                       in1=whi[:, n0 % 2, 0:width], op0=ALU.mult, op1=ALU.subtract).then_inc(lo_ready, 1)

            def lo_piece(n0, i, done):
                at_ = slice(i * CW // 4, (i + 1) * CW // 4)
                if i < 3:
                    dve.wait_ge(piece_hi, done + i + 1)
                else:
                    dve.wait_ge(hi_ready, n0 + 1)
                V.scalar_tensor_tensor(out=wlo[:, n0 % 2, at_], in0=stage[:, n0 % 2, at_], scalar=WSCALE,
                                       in1=whi[:, n0 % 2, at_], op0=ALU.mult, op1=ALU.subtract).then_inc(piece_lo if i < 3 else lo_ready, 1)

            def inverse_root(value, meanwhile=None):
                dve.wait_ge(rms_ready, value)
                V.reciprocal(irms[:, value - 1, :], rms[:, value - 1, :]).then_inc(irms_ready, 1)
                if meanwhile:
                    meanwhile()
                dve.wait_ge(rinv_ready, value)

            dve.wait_ge(vecs_landed, 16)
            for v0, v1 in ((V_POST, V_FPRE), (V_FPOST, V_BG)):
                V.tensor_scalar(vecs[:, v0:v1], vecs[:, v0:v1], UNSCALE, None, ALU.mult).then_inc(cs_ready, 1)
            dve.wait_ge(posi_ready, 1)
            for g, w in enumerate(POOL_WINDOWS):
                V.tensor_scalar(poolfix[:, g, :], posi[:, :], float(w), None, ALU.min).then_inc(dve_step, 1)
            for _ in range(4):
                step.up()
            dve.wait_ge(dve_step, step.now())
            V.reciprocal(poolfix[:, :, :], poolfix[:, :, :]).then_inc(dve_step, 1)
            dve.wait_ge(dve_step, step.up())
            for g, w in enumerate(POOL_WINDOWS):
                ins = V.tensor_scalar(poolfix[:, g, :], poolfix[:, g, :], float(w), None, ALU.mult)
                ins.then_inc(dve_step if g < 3 else posi_ready, 1)
                if g < 3:
                    step.up()
            for b in range(PAIRS):
                dve.wait_ge(sq_ready, b + 1)
                for t in range(2):
                    w = 2 * (b % 2) + t
                    if b == 0 and t == 0:
                        continue
                    ins = V.tensor_tensor(std[:, :], work[:, 0, :] if b == 0 else std[:, :], work[:, w, :], ALU.add)
                    if t == 0:
                        ins.then_inc(dve_step, 1)
                        dve.wait_ge(dve_step, step.up())
                    else:
                        ins.then_inc(sq_used, 1)
                        dve.wait_ge(sq_used, b + 1)

            def scaled(k, n):
                if k >= 4:
                    dve.wait_ge(h_lo, k - 2)
                V.tensor_tensor(work[:, k % 4:k % 4 + n, :], x_in[:, k:k + n, :],
                                rinv.unsqueeze(1).to_broadcast([P, n, S]), ALU.mult).then_inc(xr_ready, n)

            inverse_root(1, meanwhile=lambda: lo_piece(0, 0, 0))
            scaled(0, 1)
            scaled(1, 1)
            for k in range(KT):
                if k % 2 == 0 and 0 < k < KT - 2:
                    scaled(k + 2, 2)
                dve.wait_ge(xr_ready, 2 * (k // 2) + 2)
                dve.wait_ge(h_hi, k + 1)
                V.scalar_tensor_tensor(out=h[:, k, 1, :], in0=work[:, k % 4, :],
                                       scalar=vecs[:, V_PRE + k:V_PRE + k + 1], in1=h[:, k, 0, :],
                                       op0=ALU.mult, op1=ALU.subtract).then_inc(h_lo, 1)
                if k == 0:
                    scaled(2, 2)
                if k in (3, 7, 11):
                    lo_piece(0, (k + 1) // 4, 0)

            def softmax(u):
                m = u // 2
                k0 = 0 if m else P
                keys = 2 * P - k0
                pu = prob[:, u % 2, :, k0:]
                g = u % 2
                dve.wait_ge(s_done, u + 1)
                if u >= 2:
                    dve.wait_ge(pt_done, u - 1)
                bank = psum[:, 2:4, :].rearrange("p b (k j) -> p (b k) j", k=2)[:, :, k0:]
                V.scalar_tensor_tensor(out=pu, in0=bank, scalar=float(HD) ** -0.5,
                                       in1=mask[:, k0:].unsqueeze(1).to_broadcast([P, 4, keys]),
                                       op0=ALU.mult, op1=ALU.add).then_inc(s_used, 1)
                dve.wait_ge(s_used, u + 1)
                V.tensor_reduce(smax[:, 0, :], pu, AX.X, ALU.max).then_inc(dve_step, 1)
                dve.wait_ge(dve_step, step.up())
                sink = rows[:, R_SK + 4 * g:R_SK + 4 * g + 4]
                V.tensor_tensor(smax[:, 0, :], smax[:, 0, :], sink, ALU.max).then_inc(dve_step, 1)
                dve.wait_ge(dve_step, step.up())
                V.tensor_tensor(smax[:, 1, :], sink, smax[:, 0, :], ALU.subtract).then_inc(dve_step, 1)
                step.up()
                V.tensor_tensor(pu, pu, smax[:, 0, :].unsqueeze(2).to_broadcast([P, 4, keys]),
                                ALU.subtract).then_inc(s_shift, 1)
                dve.wait_ge(exp_ready, 2 * u + 2)
                V.tensor_reduce(smax[:, 2, :], pu, AX.X, ALU.add).then_inc(dve_step, 1)
                dve.wait_ge(dve_step, step.up())
                V.tensor_tensor(smax[:, 2, :], smax[:, 2, :], smax[:, 1, :], ALU.add).then_inc(dve_step, 1)
                dve.wait_ge(dve_step, step.up())
                if u >= 1:
                    dve.wait_ge(prob_ready, u)
                V.reciprocal(smax[:, 3, :], smax[:, 2, :]).then_inc(dve_step, 1)
                dve.wait_ge(dve_step, step.up())
                V.tensor_tensor(pu, pu, smax[:, 3, :].unsqueeze(2).to_broadcast([P, 4, keys]),
                                ALU.mult).then_inc(prob_ready, 1)

            def heads_low(u):
                m = u // 2
                half = HALF1 if u % 2 else HALF0
                dve.wait_ge(b_hi, u + 1)
                V.tensor_tensor(b_out[half, :, 1, m * P:m * P + P],
                                psum[half, 6, :].rearrange("p (k q) -> p k q", k=4),
                                b_out[half, :, 0, m * P:m * P + P], ALU.subtract).then_inc(b_lo, 1)

            def taps(first, last):
                for at_ in range(first, min(last, BT * CONV_W)):
                    i, q = at_ // CONV_W, at_ % CONV_W
                    tap = CONV_W - 1 - q
                    w = vecs[:, V_DW + tap * BT + i:V_DW + tap * BT + i + 1]
                    if q == 0:
                        dve.wait_ge(glu_ready, i + 1)
                        ins = V.tensor_scalar(conv[:, i, :], glu[:, i, :], w, vecs[:, V_DB + i:V_DB + i + 1],
                                              ALU.mult, ALU.add)
                    else:
                        ins = V.scalar_tensor_tensor(out=conv[:, i, q:S], in0=glu[:, i, 0:S - q], scalar=w,
                                                     in1=conv[:, i, q:S], op0=ALU.mult, op1=ALU.add)
                    if at_ == BT * CONV_W - 1:
                        ins.then_inc(conv_done, 1)
                    else:
                        ins.then_inc(dve_step, 1)
                        dve.wait_ge(dve_step, step.up())

            def value_stats(m):
                dve.wait_ge(av_done, m + 1)
                V.bn_stats(lnstat[:, m, :], psum[:, 7, :]).then_inc(dve_step, 1)
                dve.wait_ge(dve_step, step.up())
                V.bn_aggr(lnmv[:, m, :], lnstat[:, m, :]).then_inc(lnvar_ready, 1)
                dve.wait_ge(lnvar_ready, m + 1)
                V.tensor_scalar(a_vn[:, m, :], psum[:, 7, :], lnmv[:, m, 0:1], None, ALU.subtract).then_inc(av_used, 1)

            def tasks(k):
                if 2 <= k <= 13:
                    s = k // 2 - 1
                    taps(21 * s + (7 if k % 2 else 0), 21 * s + (21 if k % 2 else 7))
                if k == 15:
                    dve.wait_ge(mean_done, 1)
                    V.scalar_tensor_tensor(out=conv[:, :, :], in0=psum[:, 6, :].unsqueeze(1).to_broadcast([P, BT, S]),
                                           scalar=-1.0 / BW, in1=conv[:, :, :],
                                           op0=ALU.mult, op1=ALU.add).then_inc(centered, 1)
                if k == 17:
                    dve.wait_ge(cstd_ready, 1)
                    V.reciprocal(std[:, :], std[:, :]).then_inc(dve_step, 1)
                    dve.wait_ge(dve_step, step.up())
                    V.tensor_tensor(conv[:, :, :], conv[:, :, :], std[:, :].unsqueeze(1).to_broadcast([P, BT, S]),
                                    ALU.mult).then_inc(cnorm_ready, 1)
                if 0 <= k - 18 < 8:
                    heads_low(k - 18)
                if k == 15:
                    dve.wait_ge(rows_landed, 16)
                    dve.wait_ge(consts_ready, 4)
                if 0 <= k - 15 < 8:
                    softmax(k - 15)
                if k == 19:
                    dve.wait_ge(d_hi, 1)
                    V.tensor_tensor(d_out[:, :, 1, :], conv[:, :, :], d_out[:, :, 0, :], ALU.subtract).then_inc(d_lo, 1)
                if 0 <= k - 21 < NB:
                    value_stats(k - 21)
                if k == 26:
                    dve.wait_ge(lnstd_ready, 1)
                    V.reciprocal(lnrs[:, :], lnrs[:, :]).then_inc(dve_step, 1)
                    dve.wait_ge(dve_step, step.up())
                    for m in range(NB):
                        V.scalar_tensor_tensor(out=a_vn[:, m, :], in0=a_vn[:, m, :], scalar=lnrs[:, m:m + 1],
                                               in1=rows[:, R_VG:R_VG + BW], op0=ALU.mult, op1=ALU.mult).then_inc(dve_step, 1)
                        step.up()
                    dve.wait_ge(dve_step, step.now())
                    V.tensor_tensor(a_vn[:, :, :], a_vn[:, :, :],
                                    rows[:, R_VB:R_VB + BW].unsqueeze(1).to_broadcast([P, NB, BW]), ALU.add).then_inc(vn_ready, 1)
                if k == 28:
                    dve.wait_ge(sv_done, 1)
                    for g in range(BT):
                        bs = rows[:, R_BS + g * P:R_BS + g * P + P].unsqueeze(1).to_broadcast([P, NB, P])
                        V.tensor_tensor(a_vn[:, g, :].rearrange("p (m i) -> p m i", m=NB),
                                        psum[:, 2 + g, :].rearrange("p (m i) -> p m i", m=NB), bs, ALU.add).then_inc(dve_step, 1)
                        dve.wait_ge(dve_step, step.up())
                        V.tensor_tensor(a_u[:, g, :], a_u[:, g, :], a_vn[:, g, :], ALU.mult).then_inc(au_ready, 1)
                if k == 30:
                    dve.wait_ge(a_hi, 1)
                    V.tensor_tensor(a_out[:, :, 1, :], a_u[:, :, :], a_out[:, :, 0, :], ALU.subtract).then_inc(a_lo, 1)
                if k == 31:
                    for g, w in enumerate(POOL_WINDOWS):
                        dve.wait_ge(win_ready, g + 1)
                        V.scalar_tensor_tensor(out=c_x[:, g, :], in0=work[:, 2 * (g % 2), :], scalar=1.0 / w,
                                               in1=c_x[:, g, :], op0=ALU.mult, op1=ALU.subtract).then_inc(win_used, 1)
                if k == 33:
                    dve.wait_ge(c_hi, 1)
                    V.tensor_tensor(c_out[:, :, 1, :], c_x[:, :, :], c_out[:, :, 0, :], ALU.subtract).then_inc(c_lo, 1)

            for i in range(4):
                lo_piece(1, i, 3)
            for n in range(1, N_IN):
                tasks(2 * n)
                lo(n + 1)
                tasks(2 * n + 1)

            def merge(n0, jj, next_width=CW, per_turn=0, turn=None):
                lo(n0 + 5, next_width, per_turn, turn)
                if jj >= 1:
                    dve.wait_ge(m_lo, at(2 * jj, 4, turn))
                for t in range(2):
                    acc, tmp = work[:, 2 * t, :], work[:, 2 * t + 1, :]
                    for b in range(4):
                        i = 4 * t + b
                        if i < 7:
                            dve.wait_ge(y_ready, at(7 * jj + i + 1, 14, turn))
                        else:
                            dve.wait_ge(chunk_done, at(n0 + 5, per_turn, turn))
                        if b == 2:
                            c = V_CS + 2 * jj + t
                            scale = vecs[:, c:c + 1] if turn is None else vecs[:, bass.ds(at(c, 4, turn), 1)]
                        else:
                            scale = UNSCALE
                        V.scalar_tensor_tensor(out=tmp if b else acc, in0=psum[:, 2 + i % 6, :], scalar=scale,
                                               in1=gates[:, b, t, :], op0=ALU.mult, op1=ALU.mult).then_inc(y_used, 1)
                        if b:
                            dve.wait_ge(y_used, at(8 * jj + i + 1, 16, turn))
                            ins = V.tensor_tensor(acc, acc, tmp, ALU.add)
                            if b < 3:
                                ins.then_inc(dve_step, 1)
                                dve.wait_ge(dve_step, step.up())
                            else:
                                ins.then_inc(merged_ready, 1)
                for t in range(2):
                    dve.wait_ge(merged_ready, at(2 * jj + t + 1, 4, turn))
                    dve.wait_ge(m_hi, at(2 * jj + t + 1, 4, turn))
                    j = 2 * jj + t
                    m = merged[:, j] if turn is None else \
                        merged[:, bass.ds(at(j, 4, turn), 1)].rearrange("p o l s -> p (o l) s")
                    V.tensor_tensor(m[:, 1, :], work[:, 2 * t, :], m[:, 0, :], ALU.subtract).then_inc(m_lo, 1)

            def pair_stage(n0, jj, task=None, per_turn=0, turn=None):
                for b in range(4):
                    if task:
                        tasks(2 * (n0 + b))
                    lo(n0 + b + 1, BRW if b == 3 else CW, per_turn, turn)
                    if task:
                        tasks(2 * (n0 + b) + 1)
                merge(n0, jj, CW, per_turn, turn)

            pair_stage(C_G, 0, task=True)
            with dve.Fori(0, 3) as turn:
                step.enter(turn, 8)
                pair_stage(C_G + 5, 1, None, 10, turn)
                pair_stage(C_G + 10, 2, None, 10, turn)
            step.leave(3)
            pair_stage(C_G + 35, 7)

            for n in range(2):
                lo(C_O + n + 1)
            with dve.Fori(0, PAIRS // 2 - 1) as turn:
                lo(C_O + 3, CW, 2, turn)
                lo(C_O + 4, CW, 2, turn)

            lo_piece(C_F + 1, 0, 6)
            inverse_root(2)
            dve.wait_ge(cs_ready, 2)

            scaled_mixes = Count()

            def add_mix(k, n):
                if k % 8 == 0:
                    dve.wait_ge(res_landed[k // 8], 16)
                some = slice(k, k + n)
                V.tensor_tensor(mix[:, some, :], mix[:, some, :],
                                rinv.unsqueeze(1).to_broadcast([P, n, S]), ALU.mult).then_inc(mix_scaled, 1)
                dve.wait_ge(mix_scaled, scaled_mixes.up())
                V.tensor_tensor(res[:, some, :], res[:, some, :], mix[:, some, :], ALU.add).then_inc(x2_ready, n)

            add_mix(0, 1)
            add_mix(1, 1)
            for b in range(PAIRS):
                dve.wait_ge(x2_ready, 2 * b + 2)
                for k in (2 * b, 2 * b + 1):
                    dve.wait_ge(h_hi, KT + k + 1)
                    V.scalar_tensor_tensor(out=h2[:, k, 1, :], in0=res[:, k, :],
                                           scalar=vecs[:, V_FPRE + k:V_FPRE + k + 1], in1=h2[:, k, 0, :],
                                           op0=ALU.mult, op1=ALU.subtract).then_inc(h_lo, 1)
                if b == 0:
                    add_mix(2, 2)
                if b + 2 < PAIRS:
                    add_mix(2 * b + 4, 2)
                if b in (1, 3, 5):
                    lo_piece(C_F + 1, (b + 1) // 2, 6)
            inverse_root(3)
            V.tensor_copy(rinv_sb[:, :], rinv).then_inc(rinv_copied, 1)
            dve.wait_ge(rinv_copied, 1)

            def ffn_chunk(n0, j0, width, turn):
                if n0 > C_F + 1:
                    lo(n0 + 1, width, 2, turn)
                w = 2 * ((n0 - C_F) % 2)
                bank = 2 if n0 == C_F + 1 else 0
                if j0 >= 2:
                    dve.wait_ge(f_lo, at(j0 - 1, 2, turn))
                if n0 > C_F + 1:
                    dve.wait_ge(tile0_done, at(E_F + j0 + 1, 2, turn))
                else:
                    dve.wait_ge(chunk_done, n0 + 1)
                V.tensor_tensor(work[:, w, :], psum[:, bank, :], rinv_sb[:, :], ALU.mult).then_inc(evicted0, 1)
                if n0 > C_F + 1:
                    dve.wait_ge(chunk_done, at(n0 + 1, 2, turn))
                V.scalar_tensor_tensor(out=work[:, w + 1, :], in0=psum[:, bank + 1, :], scalar=UNSCALE, in1=rinv_sb[:, :],
                                       op0=ALU.mult, op1=ALU.mult).then_inc(evicted1, 1)
                if n0 == C_F:
                    for i in range(4):
                        lo_piece(C_F + 2, i, 9)
                dve.wait_ge(evicted1, at(E_F + j0 + 1, 2, turn))
                dve.wait_ge(f_silu, at(j0 + 1, 2, turn))
                V.tensor_tensor(work[:, w, :], work[:, w, :], work[:, w + 1, :], ALU.mult).then_inc(f_ready, 1)
                if n0 == C_F:
                    dve.wait_ge(x2_spilled, 64)
                dve.wait_ge(f_ready, at(j0 + 1, 2, turn))
                dve.wait_ge(f_hi, at(j0 + 1, 2, turn))
                j = at(j0, 2, turn)
                fj = f[:, j] if turn is None else f[:, bass.ds(j, 1)].rearrange("p o l s -> p (o l) s")
                V.tensor_tensor(fj[:, 1, :], work[:, w, :], fj[:, 0, :], ALU.subtract).then_inc(f_lo, 1)

            ffn_chunk(C_F, 0, CW, None)
            ffn_chunk(C_F + 1, 1, CW, None)
            with dve.Fori(0, FT // 2 - 2) as turn:
                ffn_chunk(C_F + 2, 2, CW, turn)
                ffn_chunk(C_F + 3, 3, CW, turn)
            ffn_chunk(C_X - 2, FT - 2, CW, None)
            ffn_chunk(C_X - 1, FT - 1, OW, None)

            with dve.Fori(0, PAIRS - 1) as turn:
                for c in range(OC):
                    lo(C_X + c + 1, OW, OC, turn)
            for c in range(OC - 1):
                lo(C_END - OC + c + 1, OW)

            inverse_root(4)
            for i, b in enumerate(b for both in zip(DVE_PAIRS, PE_PAIRS) for b in both):
                two = slice(2 * b, 2 * b + 2)
                V.tensor_tensor(ffn[:, two, :], ffn[:, two, :],
                                rinv.unsqueeze(1).to_broadcast([P, 2, S]), ALU.mult).then_inc(y_scaled, 1)
                if b in DVE_PAIRS:
                    dve.wait_ge(x2_landed[0], 16)
                    dve.wait_ge(y_scaled, i + 1)
                    V.tensor_tensor(x2_back[:, two, :], x2_back[:, two, :], ffn[:, two, :], ALU.add).then_inc(y_out, 1)

        @block.tensor
        def _(pe):
            mm = nc.tensor.matmul

            def three(bank, w_at, slot, hk, start, stop):
                high = whi[:, slot, w_at:w_at + P]
                mm(psum[:, bank, :], high, hk[0], start=start, stop=False)
                mm(psum[:, bank, :], high, hk[1], start=False, stop=False)
                return mm(psum[:, bank, :], wlo[:, slot, w_at:w_at + P], hk[0], start=False, stop=stop)

            def gemm(n0, e0, src, per_turn=0, turn=None, e_per_turn=0, kts=KT, k_from=0,
                     start=True, stop=True, middle=None, ready=None):
                slot = n0 % 2
                if n0 not in (1, C_F + 2):
                    pe.wait_ge(lo_ready, at(n0 + 1, per_turn, turn))
                for t in range(2):
                    if start and e0 >= 1:
                        pe.wait_ge(evicted1 if t else evicted0, at(e0, e_per_turn, turn))
                    for k in range(kts):
                        if ready and t == 0:
                            ready(k)
                        hk = (src[:, k_from + k, 0, :], src[:, k_from + k, 1, :])
                        last = three(t, (2 * k + t) * P, slot, hk, start and k == 0, stop and k == kts - 1)
                    if t == 0:
                        if stop:
                            last.then_inc(tile0_done, 1)
                        if middle:
                            middle()
                    else:
                        last.then_inc(chunk_done, 1)

            def keep_clock(n):
                for _ in range(n):
                    mm(psum[:, 4, 0:P], ones[:, :], ident[:, :], start=True, stop=True)

            def gathered_sums(done):
                for m in range(NB):
                    last = mm(psum[:, 7, m:m + 1], std[:, m * P:m * P + P], ones[:, 0:1], start=True, stop=True)
                last.then_inc(done, 1)

            def spread(i, bank=6):
                pe.wait_ge(irms_ready, i + 1)
                for m in range(NB):
                    last = mm(psum[:, bank, m * P:m * P + P], irms[:, i, m:m + 1].to_broadcast([P, P]), ident[:, :],
                              start=True, stop=True)
                last.then_inc(rinv_ready, 1)

            def first_chunk():
                for k in range(KT):
                    if k == 3 * KT // 4:
                        pe.wait_ge(lo_ready, 1)
                    elif k % 4 == 0:
                        pe.wait_ge(piece_lo, k // 4 + 1)
                    pe.wait_ge(h_lo, k + 1)
                    for t in range(2):
                        last = three(t, (2 * k + t) * P, 0, (h[:, k, 0, :], h[:, k, 1, :]), k == 0, k == KT - 1)
                        if k == KT - 1:
                            last.then_inc(chunk_done if t else tile0_done, 1)

            def first_ffn_chunks():
                pe.wait_ge(lo_ready, C_F + 1)
                pe.wait_ge(evicted0, E_F)
                pe.wait_ge(evicted1, E_F)
                chunks = (C_F, C_F + 1)
                for k, n in ([(k, n) for k in range(FFN_TURNS) for n in chunks] +
                             [(k, n) for n in chunks for k in range(FFN_TURNS, KT)]):
                    if n == C_F:
                        pe.wait_ge(h_lo, KT + k + 1)
                    elif k == 3 * KT // 4:
                        pe.wait_ge(lo_ready, C_F + 2)
                    elif k % 4 == 0:
                        pe.wait_ge(piece_lo, 6 + k // 4 + 1)
                    for t in range(2):
                        last = three(2 * (n - C_F) + t, (2 * k + t) * P, n % 2, (h2[:, k, 0, :], h2[:, k, 1, :]),
                                     k == 0, k == KT - 1)
                        if k == KT - 1:
                            last.then_inc(chunk_done if t else tile0_done, 1)
                    if k == KT - 1 and n == C_F:
                        pe.wait_ge(x2sq_used, PAIRS)
                        gathered_sums(sum_ready)
                    if k == FFN_TURNS + 1 and n == C_F + 1:
                        spread(2)

            def scores(u):
                m, g = u // 2, u % 2
                half = HALF1 if g else HALF0
                k0 = 0 if m else P
                if u >= 1:
                    pe.wait_ge(s_used, u)
                for p in range(4):
                    last = mm(psum[:, 2 + p // 2, (p % 2) * 2 * P + k0:(p % 2) * 2 * P + 2 * P],
                              query[half, p, m * P:m * P + P], key[half, (m - 1) * P + k0:m * P + P], start=True, stop=True)
                last.then_inc(s_done, 1)

            def prob_transposes(u):
                m0 = 0 if u >= 2 else 1
                pe.wait_ge(prob_ready, u + 1)
                if u >= 1:
                    pe.wait_ge(pt_ready, u)
                for kb in range(m0, 2):
                    for p in range(4):
                        last = nc.tensor.transpose(psum[:, 4 + kb, p * P:p * P + P], prob[:, u % 2, p, kb * P:kb * P + P], ident[:, :])
                last.then_inc(pt_done, 1)

            def heads(u):
                m, g = u // 2, u % 2
                half = HALF1 if g else HALF0
                pe.wait_ge(pt_ready, u + 1)
                if u == 0:
                    pe.wait_ge(vt_ready, 1)
                    pe.wait_ge(cstd_ready, 1)
                else:
                    pe.wait_ge(b_lo, u)
                m0 = 0 if m else 1
                for kb in range(m0, 2):
                    last = mm(psum[half, 6, :], val_tok[:, m - 1 + kb, g * HD:g * HD + HD], prob_t[:, u % 2, kb, :],
                              start=(kb == m0), stop=(kb == 1))
                last.then_inc(pv_done, 1)

            def tasks(k):
                if k == 15:
                    pe.wait_ge(conv_done, 1)
                    for i in range(BT):
                        last = mm(psum[:, 6, :], ones[:, :], conv[:, i, :], start=(i == 0), stop=(i == BT - 1))
                    last.then_inc(mean_done, 1)
                    pe.wait_ge(evicted1, C_B + 3)
                    for m in range(NB):
                        last = nc.tensor.transpose(psum[:, 7, m * P:m * P + P], val[:, m * P:m * P + P], ident[:, :])
                    last.then_inc(vt_done, 1)
                if k == 17:
                    pe.wait_ge(csq_ready, 1)
                    for i in range(BT):
                        last = mm(psum[:, 6, :], ones[:, :], work[:, i, :], start=(i == 0), stop=(i == BT - 1))
                    last.then_inc(var_done, 1)
                if 0 <= k - 15 < 8:
                    scores(k - 15)
                if 0 <= k - 17 < 8:
                    prob_transposes(k - 17)
                if 0 <= k - 18 < 8:
                    heads(k - 18)
                if 0 <= k - 21 < NB:
                    m = k - 21
                    if m == 0:
                        pe.wait_ge(evicted1, C_AV + 2)
                        pe.wait_ge(vt_ready, 1)
                    else:
                        pe.wait_ge(av_used, m)
                    for i in range(BT):
                        last = nc.tensor.transpose(psum[:, 7, i * P:i * P + P], a_v[:, i, m * P:m * P + P], ident[:, :])
                    last.then_inc(av_done, 1)
                if k == 28:
                    pe.wait_ge(vn_ready, 1)
                    pe.wait_ge(wst_masked, 1)
                    pe.wait_ge(pt_ready, 8)
                    for g in range(BT):
                        for m in range(NB):
                            last = mm(psum[:, 2 + g, m * P:m * P + P], a_vn[:, m, g * P:g * P + P], wst[:, g, :], start=True, stop=True)
                    last.then_inc(sv_done, 1)

            def branch(n0, jj, per_turn=0, turn=None):
                slot = n0 % 2
                pe.wait_ge(lo_ready, at(n0 + 1, per_turn, turn))
                for t in range(2):
                    for b, (src, w0, kts) in enumerate(((a_out, 0, BT), (b_out, BT, BT), (c_out, 3 * BT, 1), (d_out, 2 * BT, BT))):
                        i = 4 * t + b
                        if i >= 6:
                            pe.wait_ge(y_used, at(8 * jj + i - 5, 16, turn))
                        elif jj >= 1:
                            pe.wait_ge(y_used, at(8 * jj, 16, turn))
                        for k in range(kts):
                            if b == 2:
                                g = jj // 2
                                hk = [src[:, g, l, :] if turn is None else
                                      src[:, bass.ds(at(g, 1, turn), 1), l, :].rearrange("p o s -> p (o s)") for l in range(2)]
                            else:
                                hk = (src[:, k, 0, :], src[:, k, 1, :])
                            last = three(2 + i % 6, (2 * (w0 + k) + t) * P, slot, hk, k == 0, k == kts - 1)
                        last.then_inc(y_ready if i < 7 else chunk_done, 1)

            pe.wait_ge(consts_ready, 4)
            pe.wait_ge(ident_ready, 1)
            for b in range(2, PAIRS):
                pe.wait_ge(sq_used, b + 1)
                if b < PAIRS - 1:
                    keep_clock(4)
            gathered_sums(sum_ready)
            spread(0)
            keep_clock(6)
            first_chunk()

            def pieces_of_chunk_1(k):
                if k == 3 * KT // 4:
                    pe.wait_ge(lo_ready, 2)
                elif k % 4 == 0:
                    pe.wait_ge(piece_lo, 3 + k // 4 + 1)

            for n in range(1, N_IN):
                gemm(n, n, h, middle=lambda: tasks(2 * n + 1), ready=pieces_of_chunk_1 if n == 1 else None)
                tasks(2 * n + 2)
            for b in range(4):
                n = C_G + b
                gemm(n, n, h, middle=lambda: tasks(2 * n + 1))
                tasks(2 * n + 2)
            pe.wait_ge(a_lo, 1)
            pe.wait_ge(b_lo, 8)
            pe.wait_ge(c_lo, 1)
            pe.wait_ge(d_lo, 1)
            branch(C_G + 4, 0)

            def pair_stage(n0, e0, jj, per_turn=0, turn=None):
                for b in range(4):
                    gemm(n0 + b, e0 + b, h, per_turn, turn, 8)
                branch(n0 + 4, jj, per_turn, turn)

            with pe.Fori(0, 3) as turn:
                pair_stage(C_G + 5, E_G + 4, 1, 10, turn)
                pair_stage(C_G + 10, E_G + 8, 2, 10, turn)
            pair_stage(C_G + 35, E_G + 28, 7)

            def merged_ready_at(k):
                pe.wait_ge(m_lo, k + 1)

            gemm(C_O, E_O, merged, ready=merged_ready_at)
            gemm(C_O + 1, E_O + 1, merged)
            with pe.Fori(0, PAIRS // 2 - 1) as turn:
                for t in range(2):
                    gemm(C_O + 2 + t, E_O + 2 + t, merged, 2, turn, 2)
            keep_clock(8)
            pe.wait_ge(osq_used, PAIRS)
            gathered_sums(osum_ready)
            spread(1)
            keep_clock(12)
            first_ffn_chunks()

            def pieces_of_third_ffn_chunk(k):
                if k == 3 * KT // 4:
                    pe.wait_ge(lo_ready, C_F + 3)
                elif k % 4 == 0:
                    pe.wait_ge(piece_lo, 9 + k // 4 + 1)

            gemm(C_F + 2, E_F + 1, h2, ready=pieces_of_third_ffn_chunk)
            gemm(C_F + 3, E_F + 3, h2)
            with pe.Fori(0, FT // 2 - 2) as turn:
                for t in range(2):
                    gemm(C_F + 4 + t, E_F + 4 + t, h2, 2, turn, 2)
            with pe.Fori(0, PAIRS) as turn:
                for c in range(OC):
                    pe.wait_ge(f_lo, OK * (c + 1))
                    gemm(C_X + c, E_X, f, OC, turn, 1, kts=OK, k_from=OK * c, start=(c == 0), stop=(c == OC - 1))

            def bring_x2(i):
                mm(psum[:, PE_BANKS[i], :], ident[:, :], x2_back[:, 2 * PE_PAIRS[0] + i, :], start=True, stop=False)

            pe.wait_ge(x2_landed[0], 16)
            pe.wait_ge(x2_landed[1], 16)
            bring_x2(2)
            bring_x2(3)
            pe.wait_ge(osq_used, 2 * PAIRS)
            gathered_sums(osum_ready)
            bring_x2(4)
            spread(3)
            spread(3, bank=5)
            pe.wait_ge(evicted0, E_X + PAIRS)
            pe.wait_ge(evicted1, E_X + PAIRS)
            for i in (0, 1, 5):
                bring_x2(i)
            for i, bank in enumerate(PE_BANKS):
                pe.wait_ge(y_scaled, 2 * (i // 2) + 2)
                mm(psum[:, bank, :], ident[:, :], ffn[:, 2 * PE_PAIRS[0] + i, :], start=False, stop=True).then_inc(y_sum, 1)


def _chunks(w, order):
    k = w.shape[0] // P
    w = w[:, order].reshape(k, P, -1, 2 * P)
    return np.ascontiguousarray(w.transpose(2, 1, 0, 3)).reshape(-1, P, k * 2 * P)


def kernel(**inputs):
    from concourse import bacc
    from concourse.bass_utils import run_bass_kernel_spmd

    a = {k: np.asarray(v) for k, v in inputs.items()}
    cols = np.arange
    o_b, o_c, o_d = 2 * BW, 2 * BW + 768, 2 * BW + 768 + BW
    order = [np.r_[o_d + i * P:o_d + i * P + P, o_d + BW + i * P:o_d + BW + i * P + P] for i in range(BT)]
    heads = np.concatenate([np.r_[p * HD:p * HD + HD, (p + 4) * HD:(p + 4) * HD + HD] for p in range(4)])
    order += [o_b + heads, cols(o_b + BW, o_c), cols(BW, 2 * BW), cols(0, BW), cols(o_c, o_d)]
    w_in = _chunks(a["w_in"][0], np.concatenate(order))
    every = cols(D)
    w_gate = np.stack([_chunks(a["w_gate"][0, b], every) for b in range(4)], axis=1)
    w_a, w_b, w_d = (_chunks(a[n][0][r], every) for n, r in
                     (("a_w_out", cols(BW)), ("b_w_out", heads), ("d_w_out", cols(BW))))
    w_c = a["c_w_map"][0].reshape(BT, P, 2, 2 * P).transpose(0, 2, 1, 3).reshape(PAIRS, P, 2 * P)
    w_branch = np.concatenate([w_a, w_b, w_d, w_c], axis=2)
    w_o = _chunks(a["w_o"][0], every)
    gu = np.concatenate([np.r_[j * P:j * P + P, DFF + j * P:DFF + j * P + P] for j in range(FT)])
    w_ffn_in = _chunks(a["w_ffn_in"][0], gu)
    w_ffn_out = a["w_ffn_out"][0].reshape(OC, OK, P, PAIRS, 2 * P).transpose(3, 0, 2, 1, 4).reshape(-1, P, OW)

    def by_tile(v):
        return v.reshape(-1, P).T

    vecs = np.concatenate([by_tile(a[n][0]) for n in (
        "norm_mix_pre", "norm_mix_post", "norm_ffn_pre", "norm_ffn_post", "c_scale", "b_gate",
        "d_w_dw", "d_b_dw", "d_ln_g", "d_ln_b")], axis=1)
    rows = np.concatenate([a[n][0].reshape(-1) for n in ("a_vnorm_g", "a_vnorm_b", "a_b_s", "b_sinks")])
    x = a["x"][0].T.reshape(KT, P, S).transpose(1, 0, 2)
    ws = a["a_w_s"][0].transpose(2, 0, 1)

    arrays = {"x_t": x, "w_in_chunks": w_in, "w_gate_chunks": w_gate, "w_branch_chunks": w_branch,
              "w_o_chunks": w_o, "w_ffn_in_chunks": w_ffn_in, "w_ffn_out_chunks": w_ffn_out,
              "vectors": vecs, "row_vectors": rows, "w_s_t": ws}
    arrays = {n: np.ascontiguousarray(v) for n, v in arrays.items()}
    nc = bacc.Bacc("TRN2", target_bir_lowering=False, num_devices=1)
    args = [nc.dram_tensor(n, v.shape, mybir.dt.from_np(v.dtype), kind="ExternalInput").ap() for n, v in arrays.items()]
    out = nc.dram_tensor("out_t", (P, KT, S), F32, kind="ExternalOutput").ap()
    x2_spill = nc.dram_tensor("x2_spill", (P, KT, S), F32).ap()
    block_program(nc, *args, out, x2_spill)
    r = run_bass_kernel_spmd(nc, [arrays], core_ids=[0])
    got = np.asarray(r.results[0]["out_t"])
    return np.ascontiguousarray(got.transpose(1, 0, 2).reshape(D, S).T)[None]
```
